# Optimizing a Trainium2 kernel written in Bass

```python
import math
import jax, jax.numpy as jnp
from jax import lax
import numpy as np

D_MODEL = 1024
BATCH = 1
SEQ = 256
DEPTH = 2

MIX_WIDTH = D_MODEL
ATT_WIDTH = MIX_WIDTH // 2
FOURIER_WIDTH = MIX_WIDTH - ATT_WIDTH
N_HEADS = 8
HEAD_DIM = ATT_WIDTH // (2 * N_HEADS)
V_HEAD_DIM = 2 * HEAD_DIM
N_FGROUPS = 4
FGROUP_DIM = FOURIER_WIDTH // N_FGROUPS
IN_COLS = 3 * ATT_WIDTH + FOURIER_WIDTH
D_FF = ((8 * D_MODEL + 3 * 256 - 1) // (3 * 256)) * 256
Q_BLOCK = 128
LN_EPS = 1e-5
SUBLN_EPS = 1e-5
ALPHA = (2.0 * DEPTH) ** 0.25
BETA = (8.0 * DEPTH) ** -0.25
LAMBDA_STD = 0.1


def layer_norm(x, g, b):
    x32 = x.astype(jnp.float32)
    mu = jnp.mean(x32, axis=-1, keepdims=True)
    var = jnp.mean(jnp.square(x32 - mu), axis=-1, keepdims=True)
    return ((x32 - mu) * lax.rsqrt(var + LN_EPS) * g + b).astype(x.dtype)

def lambda_init_fn(layer_idx):
    return 0.8 - 0.6 * math.exp(-0.3 * layer_idx)

def diff_attention(q, k, v, lam, lam_init, subln_g):
    B, S = q.shape[0], q.shape[1]
    nb = S // Q_BLOCK
    slopes = jnp.exp2(-8.0 * jnp.arange(1, N_HEADS + 1, dtype=jnp.float32) / N_HEADS)
    kpos = jnp.arange(S, dtype=jnp.float32)
    scale = HEAD_DIM ** -0.5
    qb = q.reshape(B, nb, Q_BLOCK, N_HEADS, 2, HEAD_DIM).transpose(1, 0, 2, 3, 4, 5)
    starts = jnp.arange(nb, dtype=jnp.float32) * Q_BLOCK

    def block(args):
        qi, start = args
        s = jnp.einsum('bqhcd,bkhcd->bhcqk', qi, k).astype(jnp.float32) * scale
        qpos = start + jnp.arange(Q_BLOCK, dtype=jnp.float32)
        dist = jnp.abs(qpos[:, None] - kpos[None, :])
        s = s - slopes[:, None, None, None] * dist[None, None]
        p = jax.nn.softmax(s, axis=-1)
        a = p[:, :, 0] - lam * p[:, :, 1]
        o = jnp.einsum('bhqk,bkhd->bqhd', a.astype(v.dtype), v).astype(jnp.float32)
        o = o * lax.rsqrt(jnp.mean(jnp.square(o), axis=-1, keepdims=True) + SUBLN_EPS)
        o = o * subln_g * (1.0 - lam_init)
        return o.astype(v.dtype)

    out = lax.map(block, (qb, starts))
    return out.transpose(1, 0, 2, 3, 4).reshape(B, S, N_HEADS * V_HEAD_DIM)

def fourier_mix(u, w_f, b_f):
    B, S = u.shape[0], u.shape[1]
    ug = u.reshape(B, S, N_FGROUPS, FGROUP_DIM).astype(jnp.float32)
    f = jnp.fft.fft(ug, axis=3, norm='ortho')
    f = jnp.fft.fft(f, axis=1, norm='ortho').real.astype(u.dtype)
    y = jnp.einsum('bsgc,gcd->bsgd', f, w_f)
    return y.reshape(B, S, FOURIER_WIDTH) + b_f

def swiglu(h, w_gu, w_down):
    gu = jnp.einsum('bsd,df->bsf', h, w_gu)
    g, up = gu[..., :D_FF], gu[..., D_FF:]
    return jnp.einsum('bsf,fd->bsd', jax.nn.silu(g) * up, w_down)

def first_inputs(seed: int = 0) -> dict:
    key = jax.random.key(seed)
    ks = jax.random.split(key, 16)
    f32 = jnp.float32
    nrm = lambda k, shape: jax.random.normal(k, shape, f32)
    return {
        'x': nrm(ks[0], (BATCH, SEQ, D_MODEL)),
        'ln_in_g': 1.0 + 0.01 * nrm(ks[1], (D_MODEL,)),
        'ln_in_b': 0.01 * nrm(ks[2], (D_MODEL,)),
        'w_in': nrm(ks[3], (DEPTH, D_MODEL, IN_COLS)) * D_MODEL ** -0.5,
        'lam_params': LAMBDA_STD * nrm(ks[4], (DEPTH, 4, HEAD_DIM)),
        'subln_g': 1.0 + 0.01 * nrm(ks[5], (DEPTH, V_HEAD_DIM)),
        'w_f': nrm(ks[6], (DEPTH, N_FGROUPS, FGROUP_DIM, FGROUP_DIM)) * FGROUP_DIM ** -0.5,
        'b_f': 0.01 * nrm(ks[7], (DEPTH, FOURIER_WIDTH)),
        'w_o': nrm(ks[8], (DEPTH, MIX_WIDTH, D_MODEL)) * (MIX_WIDTH ** -0.5 * BETA),
        'ln1_g': 1.0 + 0.01 * nrm(ks[9], (DEPTH, D_MODEL)),
        'ln1_b': 0.01 * nrm(ks[10], (DEPTH, D_MODEL)),
        'w_gu': nrm(ks[11], (DEPTH, D_MODEL, 2 * D_FF)) * D_MODEL ** -0.5,
        'w_down': nrm(ks[12], (DEPTH, D_FF, D_MODEL)) * (D_FF ** -0.5 * BETA),
        'ln2_g': 1.0 + 0.01 * nrm(ks[13], (DEPTH, D_MODEL)),
        'ln2_b': 0.01 * nrm(ks[14], (DEPTH, D_MODEL)),
    }

def first_block(x, ln_in_g, ln_in_b, w_in, lam_params, subln_g, w_f, b_f, w_o,
              ln1_g, ln1_b, w_gu, w_down, ln2_g, ln2_b):
    B, S = x.shape[0], x.shape[1]
    h = layer_norm(x, ln_in_g, ln_in_b)
    for l in range(DEPTH):
        lam_init = lambda_init_fn(l)
        proj = jnp.einsum('bsd,de->bse', h, w_in[l])
        q = proj[..., :ATT_WIDTH].reshape(B, S, N_HEADS, 2, HEAD_DIM)
        k = proj[..., ATT_WIDTH:2 * ATT_WIDTH].reshape(B, S, N_HEADS, 2, HEAD_DIM)
        v = proj[..., 2 * ATT_WIDTH:3 * ATT_WIDTH].reshape(B, S, N_HEADS, V_HEAD_DIM)
        u = proj[..., 3 * ATT_WIDTH:]
        lp = lam_params[l].astype(jnp.float32)
        lam = jnp.exp(jnp.sum(lp[0] * lp[1])) - jnp.exp(jnp.sum(lp[2] * lp[3])) + lam_init
        a = diff_attention(q, k, v, lam, lam_init, subln_g[l])
        f = fourier_mix(u, w_f[l], b_f[l])
        mix = jnp.einsum('bse,ed->bsd', jnp.concatenate([a, f], axis=-1), w_o[l])
        h = layer_norm(ALPHA * h + mix, ln1_g[l], ln1_b[l])
        h = layer_norm(ALPHA * h + swiglu(h, w_gu[l], w_down[l]), ln2_g[l], ln2_b[l])
    return h


DEPTH_2 = 1

N_ATTN_HEADS = 8
HEAD_DIM_2 = 64
ATTN_WIDTH = N_ATTN_HEADS * HEAD_DIM_2
N_CONV_GROUPS = 8
CONV_GROUP_DIM = 64
CONV_WIDTH = N_CONV_GROUPS * CONV_GROUP_DIM
CONV_KSIZE = 3
D_FF_2 = 2816
N_SUBLAYERS = 3
N_MOD = 3
EPS = 1e-6
FFN_RES_WEIGHT = 0.5
MIX_IN_WIDTH = 3 * CONV_WIDTH + 3 * ATTN_WIDTH + 2 * D_MODEL


def rmsnorm(x, g):
    xf = x.astype(jnp.float32)
    inv = lax.rsqrt(jnp.mean(xf * xf, axis=-1, keepdims=True) + EPS)
    return (xf * inv).astype(x.dtype) * g

def modulate(x, shift, scale):
    return x * (1 + scale[:, None, :]) + shift[:, None, :]

def swiglu_2(x, w_gu, w_down):
    g, u = jnp.split(x @ w_gu, 2, axis=-1)
    return (jax.nn.silu(g) * u) @ w_down

def short_conv(b_gate, c_gate, xin, conv_w):
    v = c_gate * xin
    S = v.shape[1]
    vp = jnp.pad(v, ((0, 0), (CONV_KSIZE - 1, 0), (0, 0)))
    y = conv_w[0] * vp[:, 0:S, :]
    for k in range(1, CONV_KSIZE):
        y = y + conv_w[k] * vp[:, k:k + S, :]
    return b_gate * y

def stick_breaking_attention(q, k, v):
    S = q.shape[2]
    scale = HEAD_DIM_2 ** -0.5
    qf = q.astype(jnp.float32)
    kf = k.astype(jnp.float32)
    vf = v.astype(jnp.float32)
    outs = []
    for i in range(S // Q_BLOCK):
        start = i * Q_BLOCK
        end = start + Q_BLOCK
        q_blk = qf[:, :, start:end, :]
        k_c = kf[:, :, :end, :]
        v_c = vf[:, :, :end, :]
        z = jnp.einsum('bhqd,bhkd->bhqk', q_blk, k_c) * scale
        t_pos = start + jnp.arange(Q_BLOCK)
        s_pos = jnp.arange(end)
        valid = s_pos[None, :] < t_pos[:, None]
        sp = jnp.where(valid, jax.nn.softplus(z), 0.0)
        rem = lax.cumsum(sp, axis=3, reverse=True) - sp
        log_a = jax.nn.log_sigmoid(z) - rem
        a = jnp.where(valid, jnp.exp(log_a), 0.0)
        outs.append(jnp.einsum('bhqk,bhkd->bhqd', a, v_c))
    return jnp.concatenate(outs, axis=2).astype(q.dtype)

def mixer(u, w_mix_in, b_merge, conv_w, w_conv_out, w_attn_out, w_out):
    B, S, _ = u.shape
    proj = u @ w_mix_in
    idx = [CONV_WIDTH, 2 * CONV_WIDTH, 3 * CONV_WIDTH,
           3 * CONV_WIDTH + ATTN_WIDTH, 3 * CONV_WIDTH + 2 * ATTN_WIDTH,
           3 * CONV_WIDTH + 3 * ATTN_WIDTH, 3 * CONV_WIDTH + 3 * ATTN_WIDTH + D_MODEL]
    cb, cc, cx, q, k, v, ga, gb = jnp.split(proj, idx, axis=-1)
    ya = short_conv(cb, cc, cx, conv_w) @ w_conv_out
    def heads(t):
        return t.reshape(B, S, N_ATTN_HEADS, HEAD_DIM_2).transpose(0, 2, 1, 3)
    o = stick_breaking_attention(heads(q), heads(k), heads(v))
    o = o.transpose(0, 2, 1, 3).reshape(B, S, ATTN_WIDTH)
    yb = o @ w_attn_out
    merged = jax.nn.sigmoid(ga + b_merge[0]) * ya + jax.nn.sigmoid(gb + b_merge[1]) * yb
    return merged @ w_out

def second_inputs(seed: int = 0) -> dict:
    key = jax.random.key(seed)
    ks = jax.random.split(key, 24)
    f32 = jnp.float32
    L, D = DEPTH_2, D_MODEL

    def nrm(k, shape, s):
        return jax.random.normal(k, shape, f32) * s

    return {
        "x": nrm(ks[0], (BATCH, SEQ, D), 1.0),
        "c": nrm(ks[1], (BATCH, D), 1.0),
        "w_ada": nrm(ks[2], (L, D, N_SUBLAYERS * N_MOD * D), 0.5 * D ** -0.5),
        "b_ada": nrm(ks[3], (L, N_SUBLAYERS * N_MOD * D), 0.02),
        "norm1_g": 1.0 + nrm(ks[4], (L, D), 0.02),
        "ffn1_w_gu": nrm(ks[5], (L, D, 2 * D_FF_2), D ** -0.5),
        "ffn1_w_down": nrm(ks[6], (L, D_FF_2, D), D_FF_2 ** -0.5),
        "norm2_g": 1.0 + nrm(ks[7], (L, D), 0.02),
        "w_mix_in": nrm(ks[8], (L, D, MIX_IN_WIDTH), D ** -0.5),
        "b_merge": nrm(ks[9], (L, 2, D), 0.02),
        "conv_w": nrm(ks[10], (L, CONV_KSIZE, CONV_WIDTH), CONV_KSIZE ** -0.5),
        "w_conv_out": nrm(ks[11], (L, CONV_WIDTH, D), CONV_WIDTH ** -0.5),
        "w_attn_out": nrm(ks[12], (L, ATTN_WIDTH, D), ATTN_WIDTH ** -0.5),
        "w_out": nrm(ks[13], (L, D, D), D ** -0.5),
        "norm3_g": 1.0 + nrm(ks[14], (L, D), 0.02),
        "ffn2_w_gu": nrm(ks[15], (L, D, 2 * D_FF_2), D ** -0.5),
        "ffn2_w_down": nrm(ks[16], (L, D_FF_2, D), D_FF_2 ** -0.5),
        "final_g": 1.0 + nrm(ks[17], (D,), 0.02),
    }

def second_block(x, c, w_ada, b_ada, norm1_g, ffn1_w_gu, ffn1_w_down, norm2_g,
              w_mix_in, b_merge, conv_w, w_conv_out, w_attn_out, w_out,
              norm3_g, ffn2_w_gu, ffn2_w_down, final_g):
    B = x.shape[0]
    c_act = jax.nn.silu(c)
    h = x
    for l in range(DEPTH_2):
        mod = (c_act @ w_ada[l] + b_ada[l]).reshape(B, N_SUBLAYERS, N_MOD, D_MODEL)
        u = modulate(rmsnorm(h, norm1_g[l]), mod[:, 0, 0], mod[:, 0, 1])
        h = h + FFN_RES_WEIGHT * mod[:, 0, 2][:, None, :] * swiglu_2(u, ffn1_w_gu[l], ffn1_w_down[l])
        u = modulate(rmsnorm(h, norm2_g[l]), mod[:, 1, 0], mod[:, 1, 1])
        y = mixer(u, w_mix_in[l], b_merge[l], conv_w[l], w_conv_out[l], w_attn_out[l], w_out[l])
        h = h + mod[:, 1, 2][:, None, :] * y
        u = modulate(rmsnorm(h, norm3_g[l]), mod[:, 2, 0], mod[:, 2, 1])
        h = h + FFN_RES_WEIGHT * mod[:, 2, 2][:, None, :] * swiglu_2(u, ffn2_w_gu[l], ffn2_w_down[l])
    return rmsnorm(h, final_g)


def setup_inputs(seed=0):
    out = dict(first_inputs(seed))
    for name, value in second_inputs(seed + 1).items():
        if name != "x":
            out[name + "_2"] = value
    return out


def reference(
    x, ln_in_g, ln_in_b, w_in, lam_params, subln_g, w_f, b_f, w_o, ln1_g, ln1_b, w_gu, w_down,
    ln2_g, ln2_b, c_2, w_ada_2, b_ada_2, norm1_g_2, ffn1_w_gu_2, ffn1_w_down_2, norm2_g_2,
    w_mix_in_2, b_merge_2, conv_w_2, w_conv_out_2, w_attn_out_2, w_out_2, norm3_g_2,
    ffn2_w_gu_2, ffn2_w_down_2, final_g_2,
):
    x = first_block(
        x, ln_in_g, ln_in_b, w_in, lam_params, subln_g, w_f, b_f, w_o, ln1_g, ln1_b, w_gu,
        w_down, ln2_g, ln2_b,
    )
    return second_block(
        x, c_2, w_ada_2, b_ada_2, norm1_g_2, ffn1_w_gu_2, ffn1_w_down_2, norm2_g_2, w_mix_in_2,
        b_merge_2, conv_w_2, w_conv_out_2, w_attn_out_2, w_out_2, norm3_g_2, ffn2_w_gu_2,
        ffn2_w_down_2, final_g_2,
    )


_drawn_inputs = setup_inputs


def setup_inputs(seed=0):
    import zlib

    import numpy as np

    out = dict(_drawn_inputs(seed))
    spreads = {}
    factors = {'ln_in_g': 4.515,
     'ln_in_b': 3.253,
     'lam_params': 4.548,
     'subln_g': 8.0,
     'b_f': 8.0,
     'ln1_g': 3.511,
     'ln1_b': 3.409,
     'ln2_g': 3.604,
     'ln2_b': 3.498,
     'norm1_g_2': 8.0,
     'norm2_g_2': 7.262,
     'b_merge_2': 8.0,
     'norm3_g_2': 64.0,
     'final_g_2': 7.961,
     'w_attn_out_2': 3.144}
    for name, (base, spread) in spreads.items():
        noise = np.random.default_rng([zlib.crc32(name.encode()), seed]).standard_normal(out[name].shape)
        drawn = base * np.exp(spread * noise) if base else spread * noise
        out[name] = __import__('jax').numpy.asarray(drawn.astype(out[name].dtype))
    for name, factor in factors.items():
        out[name] = (out[name] * factor).astype(out[name].dtype)
    return out
```

```python
import math
from contextlib import ExitStack

import numpy as np

import concourse.bass as bass
from concourse import mybir

F32 = mybir.dt.float32
F32R = mybir.dt.float32r
BF16 = mybir.dt.bfloat16
ALU = mybir.AluOpType
ACT = mybir.ActivationFunctionType
AX_X = mybir.AxisListType.X

P = 128
S = 256
D = 1024
KT = D // P
DEPTH = 2
HEADS = 8
ATT = 512
HD = 32
VD = 64
GROUPS = 4
FF = 2816
FT = FF // (2 * P)
SLOTS = 3
CH = 2048
LAYER_CHUNKS = 8 + 4 + 3 * FT
MIX_CHUNKS = 20 + 2 + 2 + 4
N_CHUNKS = DEPTH * LAYER_CHUNKS + 2 * 3 * FT + MIX_CHUNKS
ADA_TILES = 18
ADA_STEPS = ADA_TILES // DEPTH
ALPHA = (2.0 * DEPTH) ** 0.25
LN_EPS = 1e-5
SUBLN_EPS = 1e-5
RMS_EPS = 1e-6

LN1_G, LN1_B, LN2_G, LN2_B, B_F, SUBLN, ONE_MINUS_LI, LAM_INIT, LAM_ROWS = 0, 8, 16, 24, 32, 36, 37, 38, 39
LAYER_COLS = LAM_ROWS + 4 * HD
LNI_G, LNI_B, C_COL, B_ADA, NORM_G, B_MERGE, CONV_W, FINAL_G = 0, 8, 16, 24, 96, 120, 136, 148
COMMON_COLS = FINAL_G + 8
IDENT, ONES_D, TRI, ONES, MASK, DFT_S, DFT_C = 0, 128, 256, 384, 512, 896, 1920
CONST_COLS = DFT_C + 256
DIST, SLOPES = 0, 512
CONST16_COLS = SLOPES + HEADS * P
V0, V1, Q0, K0, Q1, K1, U0, U1, O0, G0 = 0, 1, 2, 3, 4, 5, 6, 7, 8, 12


def fused_blocks(nc, xT, stream, ada, w_f, layer_params, common_params, consts32, consts16, outT):
    with ExitStack() as ctx:
        def sb(name, shape, dt=F32):
            return ctx.enter_context(nc.sbuf_tensor(name, shape, dt))

        def sem(name):
            return ctx.enter_context(nc.semaphore(name))

        raw = [sb(f"raw{i}", [P, CH]) for i in range(SLOTS)]
        w_hi = [sb(f"w_hi{i}", [P, CH], F32R) for i in range(SLOTS)]
        w_lo = [sb(f"w_lo{i}", [P, CH], F32R) for i in range(SLOTS)]
        state = sb("state", [P, KT, 2, S])
        x_hi = sb("x_hi", [P, KT, S], F32R)
        x_lo = sb("x_lo", [P, KT, S], F32R)
        mix_hi = sb("mix_hi", [P, KT, S], F32R)
        mix_lo = sb("mix_lo", [P, KT, S], F32R)
        c32 = sb("c32", [P, CONST_COLS])
        c16 = sb("c16", [P, CONST16_COLS], BF16)
        wf = sb("wf", [P, GROUPS, P])
        lp = sb("lp", [P, LAYER_COLS])
        cp = sb("cp", [P, COMMON_COLS])
        c_act = sb("c_act", [P, KT])
        mods = sb("mods", [P, 72])
        gains = sb("gains", [P, 3, KT])
        gates = sb("gates", [P, 3, KT])
        mean = sb("mean", [P, S])
        var = sb("var", [P, S])
        rstd = sb("rstd", [P, S])
        small = sb("small", [P, 128])
        ada_acc = sb("ada_acc", [P, 512])
        hid_hi = sb("hid_hi", [P, 2, S], F32R)
        hid_lo = sb("hid_lo", [P, 2, S], F32R)
        work = sb("work", [P, 14720])

        used = [0]

        def view(n, **dims):
            at = used[0]
            used[0] += n
            assert used[0] <= 14720
            return work[:, at:at + n]

        gate_act = view(2 * S)
        hidden = view(2 * S)
        ffn_end = used[0]
        used[0] = ffn_end
        qT = view(4 * S).rearrange("p (k n) -> p k n", k=4)
        kT = view(4 * S).rearrange("p (k n) -> p k n", k=4)
        v_s = view(2 * ATT).rearrange("p (m n) -> p m n", m=2)
        attn_end = used[0]
        u_s = view(2 * ATT).rearrange("p (m n) -> p m n", m=2)
        probs = view(4 * S).rearrange("p (b c n) -> p b c n", b=2, c=2)
        a_s = view(2 * S).rearrange("p (b n) -> p b n", b=2)
        aT_s = view(2 * S).rearrange("p (k n) -> p k n", k=2)
        P_s = view(2 * S)
        f_s = view(S)
        on_s = view(2 * ATT).rearrange("p (m n) -> p m n", m=2)
        ada_raw = view(KT * 512).rearrange("p (k n) -> p k n", k=KT)
        used[0] = attn_end
        gate_b = view(4 * S).rearrange("p (k n) -> p k n", k=4)
        gate_c = view(4 * S).rearrange("p (k n) -> p k n", k=4)
        branch = work[:, attn_end:attn_end + KT * S].rearrange("p (k n) -> p k n", k=KT)
        vpad = view(4 * (S + 2)).rearrange("p (k n) -> p k n", k=4)
        conv_y = view(4 * S).rearrange("p (k n) -> p k n", k=4)
        sig_a = view(KT * S).rearrange("p (k n) -> p k n", k=KT)
        sig_b = view(KT * S).rearrange("p (k n) -> p k n", k=KT)
        soft = view(2 * 384).rearrange("p (b n) -> p b n", b=2)
        remain = view(2 * 384).rearrange("p (b n) -> p b n", b=2)
        log_a = view(2 * 384).rearrange("p (b n) -> p b n", b=2)

        ident = c32[:, IDENT:IDENT + P]
        ones_over_d = c32[:, ONES_D:ONES_D + P]
        tri = c32[:, TRI:TRI + P]
        ones = c32[:, ONES:ONES + P]
        mask = c32[:, MASK:MASK + 384]
        dft_s = c32[:, DFT_S:DFT_S + 4 * S].rearrange("p (m n) -> p m n", m=2)
        cos_c = c32[:, DFT_C:DFT_C + P]
        neg_sin_c = c32[:, DFT_C + P:DFT_C + 2 * P]
        neg_max = small[:, 0:4].rearrange("p (c m) -> p c m", c=2)
        sums = small[:, 4:8].rearrange("p (b c) -> p b c", b=2)
        inv_sums = small[:, 8:12].rearrange("p (b c) -> p b c", b=2)
        row_max = small[:, 12:16].rearrange("p (c m) -> p c m", c=2)
        lam_sum, lam_exp, lam, subg = small[:, 16:18], small[:, 18:20], small[:, 20:21], small[:, 21:22]
        head_ms, head_var, head_std, head_rstd = (small[:, a:a + 16] for a in (24, 40, 56, 72))
        lam_prod = sb("lam_prod", [P, 2 * HD])

        B = [ctx.enter_context(nc.psum_tensor(f"bank{i}", [P, 512], F32)) for i in range(8)]
        STATS = B[7]
        RES = [B[4], B[5], B[2], B[3]]

        raw_landed = [sem(f"raw_landed{i}") for i in range(SLOTS)]
        hi_ready = sem("hi_ready")
        lo_ready = sem("lo_ready")
        chunk_done = sem("chunk_done")
        consts_landed = sem("consts_landed")
        common_landed = sem("common_landed")
        x_landed = sem("x_landed")
        params_landed = sem("params_landed")
        wf_landed = sem("wf_landed")
        ada_landed = sem("ada_landed")
        ada_step = sem("ada_step")
        ada_reduced = sem("ada_reduced")
        ada_kept = sem("ada_kept")
        c_act_ready = sem("c_act_ready")
        mods_step = sem("mods_step")
        proj_evac = sem("proj_evac")
        resid_done = sem("resid_done")
        squares_done = sem("squares_done")
        stats_done = sem("stats_done")
        mean_ready = sem("mean_ready")
        mean2_ready = sem("mean2_ready")
        var_raw = sem("var_raw")
        var_ready = sem("var_ready")
        std_ready = sem("std_ready")
        rstd_ready = sem("rstd_ready")
        centered = sem("centered")
        scaled = sem("scaled")
        x_hi_ready = sem("x_hi_ready")
        full_ready = sem("full_ready")
        x_ready = sem("x_ready")
        silu_done = sem("silu_done")
        hidden_ready = sem("hidden_ready")
        hid_hi_ready = sem("hid_hi_ready")
        hid_ready = sem("hid_ready")
        down_bank = sem("down_bank")
        scores_done = sem("scores_done")
        row_max_done = sem("row_max_done")
        neg_max_ready = sem("neg_max_ready")
        probs_ready = sem("probs_ready")
        inv_ready = sem("inv_ready")
        second_ready = sem("second_ready")
        a_ready = sem("a_ready")
        aT_done = sem("aT_done")
        aT_ready = sem("aT_ready")
        o_done = sem("o_done")
        lam_step = sem("lam_step")
        lam_exp_ready = sem("lam_exp_ready")
        osq_done = sem("osq_done")
        head_step = sem("head_step")
        head_std_ready = sem("head_std_ready")
        on_ready = sem("on_ready")
        onT_done = sem("onT_done")
        mix_a_hi = sem("mix_a_hi")
        mix_a_ready = sem("mix_a_ready")
        P_done = sem("P_done")
        P_ready = sem("P_ready")
        f_done = sem("f_done")
        f_ready = sem("f_ready")
        y_done = sem("y_done")
        mix_f_hi = sem("mix_f_hi")
        mix_f_ready = sem("mix_f_ready")
        z_done = sem("z_done")
        soft_step = sem("soft_step")
        soft_raw = sem("soft_raw")
        masked_ready = sem("masked_ready")
        z_read = sem("z_read")
        rem_done = sem("rem_done")
        log_a_ready = sem("log_a_ready")
        a_exp_ready = sem("a_exp_ready")
        a2_ready = sem("a2_ready")
        o2_done = sem("o2_done")
        o2_hi = sem("o2_hi")
        o2_ready = sem("o2_ready")
        pads_ready = sem("pads_ready")
        cx_evac = sem("cx_evac")
        conv_step = sem("conv_step")
        conv_hi = sem("conv_hi")
        conv_ready = sem("conv_ready")
        branch_a = sem("branch_a")
        branch_b = sem("branch_b")
        merged_done = sem("merged_done")
        merged_hi = sem("merged_hi")
        merged_ready = sem("merged_ready")
        out_ready = sem("out_ready")
        stored = sem("stored")

        def chunk(tiles, slot, kt):
            return tiles[slot][:, :].rearrange("p (k n) -> p k n", k=kt)

        def landed(t, j):
            return 16 * (t + (j // SLOTS + 1))

        MIX_T = (DEPTH * LAYER_CHUNKS + 3 * FT) // SLOTS
        FFN1_T = DEPTH * LAYER_CHUNKS // SLOTS
        assert LAYER_CHUNKS % SLOTS == 0 and (3 * FT) % SLOTS == 0
        LT = LAYER_CHUNKS // SLOTS

        block = ctx.enter_context(nc.Block())

        @block.sync
        def _(sp):
            sp.dma_start(c32[:, :], consts32).then_inc(consts_landed, 16)
            sp.dma_start(state[:, :, 0, :], xT.rearrange("(k p) n -> p k n", p=P)).then_inc(x_landed, 16)

            for s in range(SLOTS):
                sp.dma_start(raw[s][:, :], stream[s]).then_inc(raw_landed[s], 16)
            with sp.Fori(1, N_CHUNKS // SLOTS) as t:
                for s in range(SLOTS):
                    sp.wait_ge(lo_ready, 3 * t + (s - 2))
                    sp.dma_start(raw[s][:, :], stream[bass.ds(3 * t + s, 1)].rearrange("a p n -> (a p) n"))\
                      .then_inc(raw_landed[s], 16)
            for c in range(N_CHUNKS // SLOTS * SLOTS, N_CHUNKS):
                sp.wait_ge(lo_ready, c - 2)
                sp.dma_start(raw[c % SLOTS][:, :], stream[c]).then_inc(raw_landed[c % SLOTS], 16)
            for j in range(4):
                sp.wait_ge(out_ready, 2 * j + 2)
                sp.dma_start(outT[2 * j * P:(2 * j + 2) * P, :].rearrange("(k p) n -> p k n", p=P),
                             state[:, 2 * j:2 * j + 2, 1, :]).then_inc(stored, 16)
            sp.wait_ge(stored, 64)

        @block.gpsimd
        def _(pool):
            pool.dma_start(cp[:, :], common_params).then_inc(common_landed, 16)
            pool.dma_start(c16[:, :], consts16).then_inc(common_landed, 16)
            pool.dma_start(ada_raw, ada[0]).then_inc(ada_landed, 16)
            with pool.Fori(1, ADA_TILES) as a:
                pool.wait_ge(ada_step, KT * a)
                pool.dma_start(ada_raw, ada[bass.ds(a, 1)].rearrange("a p k n -> (a p) k n")).then_inc(ada_landed, 16)

        @block.tensor
        def _(pe):
            def passes(out, wh, wl, xh, xl, natural, start, stop):
                if natural:
                    pairs = ((xh, wh), (xh, wl), (xl, wh))
                else:
                    pairs = ((wh, xh), (wh, xl), (wl, xh))
                for i, (stationary, moving) in enumerate(pairs):
                    last = nc.tensor.matmul(out, stationary, moving, start=start and i == 0,
                                            stop=stop and i == 2, skip_group_check=True)
                return last

            def projection(t, j, bank, xh, xl, ks=range(KT), order=tuple(range(KT)), natural=False, before=None):
                if ks[0] == 0:
                    pe.wait_ge(lo_ready, 3 * t + (j + 1))
                wh, wl = chunk(w_hi, j % SLOTS, KT), chunk(w_lo, j % SLOTS, KT)
                for i in ks:
                    k = order[i]
                    if before is not None:
                        before(k)
                    for n in range(2):
                        cols = slice(n * P, (n + 1) * P)
                        if natural:
                            last = passes(bank[:, n * S:(n + 1) * S], wh[:, k, :], wl[:, k, :], xh[:, k, cols],
                                          xl[:, k, cols], True, i == 0 and n == 0, i == KT - 1)
                        else:
                            last = passes(bank[:, n * S:(n + 1) * S], wh[:, k, cols], wl[:, k, cols], xh[:, k, :],
                                          xl[:, k, :], False, i == 0 and n == 0, i == KT - 1)
                if ks[-1] == KT - 1:
                    last.then_inc(chunk_done, 1)

            def input_tile(n):
                return lambda k: pe.wait_ge(x_ready, 8 * n + (k + 1))

            def stats(n, j, rms):
                pe.wait_ge(squares_done, 4 * n + (j + 1))
                for k in (2 * j, 2 * j + 1):
                    if rms:
                        last = nc.tensor.matmul(STATS[:, S:2 * S], ones_over_d, state[:, k, 1, :],
                                                start=k == 0, stop=k == KT - 1, skip_group_check=True)
                    else:
                        last = nc.tensor.matmul(STATS[:, :], ones_over_d,
                                                state[:, k, :, :].rearrange("p a n -> p (a n)"),
                                                start=k == 0, stop=k == KT - 1, skip_group_check=True)
                if j == 3:
                    last.then_inc(stats_done, 1)

            def ffn_down(t, j, step, first=False, last_step=False, n_out=None, rms=False):
                pe.wait_ge(lo_ready, 3 * t + (j + 1))
                pe.wait_ge(hid_ready, step + 1)
                wh, wl = chunk(w_hi, j % SLOTS, 2), chunk(w_lo, j % SLOTS, 2)
                for n in range(KT):
                    cols = slice(n * P, (n + 1) * P)
                    for k in range(2):
                        last = passes(RES[n // 2][:, (n % 2) * S:(n % 2 + 1) * S], wh[:, k, cols], wl[:, k, cols],
                                      hid_hi[:, k, :], hid_lo[:, k, :], False, first and k == 0 and n % 2 == 0,
                                      last_step and k == 1)
                    if last_step and n % 2 == 1 and n < KT - 1:
                        last.then_inc(down_bank, 1)
                        if n > 1:
                            stats(n_out, n // 2 - 1, rms)
                last.then_inc(chunk_done, 1)
                if last_step:
                    stats(n_out, 2, rms)
                    stats(n_out, 3, rms)

            def ffn(t, j, f, n_in, n_out, rms, with_ada):
                def gate_up(t, j, i):
                    pe.wait_ge(silu_done, FT * f + i)
                    projection(t, j, B[0], x_hi, x_lo)
                    pe.wait_ge(hidden_ready, FT * f + i)
                    projection(t, j + 1, B[1], x_hi, x_lo)

                projection(t, j, B[0], x_hi, x_lo, before=input_tile(n_in))
                projection(t, j + 1, B[1], x_hi, x_lo)
                gate_up(t, j + 2, 1)
                ffn_down(t, j + 4, FT * f, first=True)
                with pe.Fori(0, FT - 2) as i:
                    gate_up(t + i, j + 5, i + 2)
                    ffn_down(t + i, j + 7, FT * f + i + 1)
                    if with_ada:
                        pe.wait_ge(ada_step, KT * ADA_STEPS * f + KT * i + KT)
                        for q in range(4):
                            last = nc.tensor.matmul(B[6][:, q:q + 1], ada_acc[:, q * P:(q + 1) * P], ones[:, 0:1],
                                                    start=True, stop=True, skip_group_check=True)
                        last.then_inc(ada_reduced, 1)
                ffn_down(t, j + 3 * FT - 1, FT * f + (FT - 1), last_step=True, n_out=n_out, rms=rms)

            pe.wait_ge(consts_landed, 16)
            pe.wait_ge(common_landed, 32)
            for j in range(4):
                stats(0, j, False)

            with pe.Fori(0, DEPTH) as l:
                t = LT * l

                def scores(h):
                    for c in range(2):
                        if h >= 1:
                            pe.wait_ge(probs_ready, 16 * l + (2 * h - 1 + c))
                        bank = B[2 + c]
                        nc.tensor.matmul(bank[:, :], c16[:, SLOPES + h * P:SLOPES + (h + 1) * P],
                                         c16[:, DIST:DIST + 2 * S], start=True, stop=False, skip_group_check=True)
                        r = HD * (2 * (h % 2) + c)
                        for m in range(2):
                            last = nc.tensor.matmul(bank[:, m * S:(m + 1) * S],
                                                    qT[r:r + HD, h // 2, m * P:(m + 1) * P],
                                                    kT[r:r + HD, h // 2, :], start=False, stop=True,
                                                    skip_group_check=True)
                        last.then_inc(scores_done, 1)

                def transpose_a(h):
                    if h >= 1:
                        pe.wait_ge(aT_ready, 8 * l + h)
                    for m in range(2):
                        pe.wait_ge(a_ready, 16 * l + (2 * h + m + 1))
                        for kk in range(2):
                            last = nc.tensor.transpose(B[6][:, kk * S + m * P:kk * S + (m + 1) * P],
                                                       a_s[:, m, kk * P:(kk + 1) * P], ident)
                    last.then_inc(aT_done, 1)

                def values(h):
                    pe.wait_ge(aT_ready, 8 * l + (h + 1))
                    for m in range(2):
                        for kk in range(2):
                            last = nc.tensor.matmul(B[4 + m][:, h * VD:(h + 1) * VD], aT_s[:, kk, m * P:(m + 1) * P],
                                                    v_s[:, kk, h * VD:(h + 1) * VD], start=kk == 0, stop=kk == 1,
                                                    skip_group_check=True)
                    last.then_inc(o_done, 1)

                def fourier_tokens(g):
                    if g >= 1:
                        pe.wait_ge(P_ready, 4 * l + g)
                    for m in range(2):
                        last = nc.tensor.matmul(B[7][:, :], u_s[:, m, g * P:(g + 1) * P], dft_s[:, m, :],
                                                start=m == 0, stop=m == 1)
                    last.then_inc(P_done, 1)

                def fourier_features(g):
                    pe.wait_ge(P_ready, 4 * l + (g + 1))
                    if g >= 1:
                        pe.wait_ge(f_ready, 4 * l + g)
                    nc.tensor.matmul(B[0][:, 0:S], cos_c, P_s[:, 0:S], start=True, stop=False)
                    nc.tensor.matmul(B[0][:, 0:S], neg_sin_c, P_s[:, S:2 * S], start=False, stop=True)\
                        .then_inc(f_done, 1)

                def fourier_weights(g):
                    pe.wait_ge(f_ready, 4 * l + (g + 1))
                    if g >= 1:
                        pe.wait_ge(mix_f_ready, 4 * l + g)
                    nc.tensor.matmul(B[1][:, 0:S], wf[:, g, :], f_s, start=True, stop=True).then_inc(y_done, 1)

                def transpose_o(m):
                    pe.wait_ge(on_ready, 2 * l + (m + 1))
                    for e in range(4):
                        last = nc.tensor.transpose(B[2 + m][:, e * P:(e + 1) * P], on_s[:, m, e * P:(e + 1) * P],
                                                   ident)
                    last.then_inc(onT_done, 1)

                projection(t, V0, B[0], x_hi, x_lo, natural=True,
                           before=lambda k: pe.wait_ge(x_ready, 16 * l + (k + 1)))
                projection(t, V1, B[1], x_hi, x_lo, natural=True)
                for j in (Q0, K0):
                    pe.wait_ge(proj_evac, 8 * l + (j - 1))
                    projection(t, j, B[j % 2], x_hi, x_lo)
                for s in range(8):
                    j = Q1 + s // 2
                    if s >= 2:
                        transpose_a(s - 2)
                    if s % 2 == 0:
                        pe.wait_ge(proj_evac, 8 * l + (j - 1))
                    projection(t, j, B[j % 2], x_hi, x_lo, ks=range(4 * (s % 2), 4 * (s % 2) + 4),
                               natural=j in (U0, U1))
                    if s >= 2:
                        values(s - 2)
                    if s == 0:
                        pe.wait_ge(proj_evac, 8 * l + 4)
                    if s == 4:
                        pe.wait_ge(proj_evac, 8 * l + 6)
                    scores(s)
                transpose_a(6)
                pe.wait_ge(proj_evac, 8 * l + 8)
                fourier_tokens(0)
                values(6)
                fourier_tokens(1)
                transpose_a(7)
                fourier_features(0)
                values(7)
                fourier_tokens(2)
                fourier_features(1)
                pe.wait_ge(wf_landed, 16 * l + 16)
                fourier_weights(0)
                fourier_tokens(3)
                fourier_features(2)
                fourier_weights(1)
                fourier_features(3)
                fourier_weights(2)
                transpose_o(0)
                fourier_weights(3)
                transpose_o(1)

                def mixed_tile(k):
                    if k >= 4:
                        pe.wait_ge(mix_f_ready, 4 * l + (k - 3))
                    else:
                        pe.wait_ge(mix_a_ready, 2 * l + 2)

                for j in range(4):
                    projection(t, O0 + j, RES[j], mix_hi, mix_lo, order=(4, 5, 6, 7, 0, 1, 2, 3),
                               before=mixed_tile if j == 0 else None)
                    if j >= 1:
                        stats(2 * l + 1, j - 1, False)
                stats(2 * l + 1, 3, False)

                ffn(t, G0, l, 2 * l + 1, 2 * l + 2, False, True)

            for j in range(4):
                stats(5, j, True)
            ffn(FFN1_T, 0, 2, 5, 6, True, False)

            t = MIX_T
            EV = 8 * DEPTH

            def z_scores(h):
                if h >= 2:
                    pe.wait_ge(z_read, h - 1)
                r = VD * (h % 2)
                q, k = qT[r:r + VD, h // 2, :], kT[r:r + VD, h // 2, :]
                bank = B[2 + h % 2]
                nc.tensor.matmul(bank[:, 0:S], k[:, 0:P], q, start=True, stop=True, skip_group_check=True)
                nc.tensor.matmul(bank[:, S:S + P], k[:, P:S], q[:, P:S], start=False, stop=True,
                                 skip_group_check=True).then_inc(z_done, 1)

            def remainders(h):
                pe.wait_ge(masked_ready, h + 1)
                if h >= 2:
                    pe.wait_ge(log_a_ready, h - 1)
                bank, sp_ = B[4 + h % 2], soft[:, h % 2, :]
                nc.tensor.matmul(bank[:, 0:S], tri, sp_[:, 0:S], start=True, stop=False, skip_group_check=True)
                nc.tensor.matmul(bank[:, P:S], ones, sp_[:, S:S + P], start=False, stop=True, skip_group_check=True)
                nc.tensor.matmul(bank[:, S:S + P], tri, sp_[:, S:S + P], start=False, stop=True,
                                 skip_group_check=True).then_inc(rem_done, 1)

            def values2(h):
                pe.wait_ge(a2_ready, h + 1)
                if h % 2 == 0 and h >= 4:
                    pe.wait_ge(o2_ready, h // 2 - 1)
                r = VD * (h % 2)
                out = B[6 + h // 2 % 2][r:r + VD, :]
                nc.tensor.matmul(out[:, 0:S], v_s[:, 0, h * VD:(h + 1) * VD], log_a[:, h % 2, 0:S], start=True,
                                 stop=False, skip_group_check=True)
                nc.tensor.matmul(out[:, P:S], v_s[:, 1, h * VD:(h + 1) * VD], log_a[:, h % 2, S:S + P], start=False,
                                 stop=True, skip_group_check=True).then_inc(o2_done, 1)

            for j in range(20):
                if 2 <= j < 12:
                    pe.wait_ge(proj_evac, EV + j - 1)
                elif 12 <= j < 14:
                    pe.wait_ge(cx_evac, j - 11)
                elif j >= 14:
                    pe.wait_ge(proj_evac, EV + j - 3)
                if j < 6 or j >= 12:
                    projection(t, j, B[j % 2], x_hi, x_lo, natural=j < 2, before=input_tile(6) if j == 0 else None)
                    continue
                for part in range(2):
                    h = 2 * (j - 6) + part
                    projection(t, j, B[j % 2], x_hi, x_lo, ks=range(4 * part, 4 * part + 4))
                    if h == 0:
                        pe.wait_ge(proj_evac, EV + 6)
                    if 1 <= h <= HEADS:
                        remainders(h - 1)
                    if h < HEADS:
                        z_scores(h)
                    if 2 <= h < HEADS + 2:
                        values2(h - 2)

            def out_projection(j, banks, xh, xl, first_tile, ready):
                pe.wait_ge(lo_ready, 3 * t + (j + 1))
                wh, wl = chunk(w_hi, (j) % SLOTS, 4), chunk(w_lo, (j) % SLOTS, 4)
                for k in range(4):
                    ready(k)
                    for n in range(4):
                        cols = slice(n * P, (n + 1) * P)
                        last = passes(banks[n // 2][:, (n % 2) * S:(n % 2 + 1) * S], wh[:, k, cols], wl[:, k, cols],
                                      xh[:, first_tile + k, :], xl[:, first_tile + k, :], False,
                                      k == 0 and n % 2 == 0, k == 3)
                last.then_inc(chunk_done, 1)

            for j, banks in ((20, B[2:4]), (21, B[4:6])):
                out_projection(j, banks, mix_hi, mix_lo, 4, lambda k: pe.wait_ge(conv_ready, k + 1))
            for j, banks in ((22, B[6:8]), (23, B[0:2])):
                if j == 23:
                    pe.wait_ge(proj_evac, EV + 18)
                out_projection(j, banks, mix_hi, mix_lo, 0, lambda k: pe.wait_ge(o2_ready, k + 1))
            for j in range(4):
                projection(t, 24 + j, RES[j], x_hi, x_lo,
                           before=(lambda k: pe.wait_ge(merged_ready, k // 2 + 1)) if j == 0 else None)
                if j >= 1:
                    stats(7, j - 1, True)
            stats(7, 3, True)
            ffn(MIX_T, MIX_CHUNKS, 3, 7, 8, True, False)

        @block.scalar
        def _(act):
            def split(t, j, first=False):
                act.wait_ge(raw_landed[j % SLOTS], landed(t, j))
                if not first:
                    act.wait_ge(chunk_done, 3 * t + (j - 2))
                nc.scalar.activation(w_hi[j % SLOTS][:, :], raw[j % SLOTS][:, :], ACT.Copy).then_inc(hi_ready, 1)

            def squares(n, j, ready):
                ready(j)
                nc.scalar.activation(state[:, 2 * j:2 * j + 2, 1, :], state[:, 2 * j:2 * j + 2, 0, :], ACT.Square)\
                    .then_inc(squares_done, 1)

            def after_residual(m):
                return lambda j: act.wait_ge(resid_done, 4 * m + (j + 1))

            def norm(n, shift, full):
                act.wait_ge(var_ready, n + 1)
                nc.scalar.activation(rstd[:, :], var[:, :], ACT.Sqrt).then_inc(std_ready, 1)
                for k in range(KT):
                    act.wait_ge(scaled, 8 * n + (k + 1))
                    nc.scalar.activation(x_hi[:, k, :], state[:, k, 1, :], ACT.Identity, bias=shift(k))\
                        .then_inc(x_hi_ready, 1)
                    if full:
                        nc.scalar.activation(state[:, k, 0, :], state[:, k, 1, :], ACT.Identity, bias=shift(k))\
                            .then_inc(full_ready, 1)

            def ffn(t, j, f, final=False):
                def after_gate(t, j, step, first=False):
                    act.wait_ge(chunk_done, 3 * t + (j + 1))
                    if not first:
                        act.wait_ge(hidden_ready, step)
                    nc.scalar.activation(gate_act, B[0][:, :], ACT.Silu).then_inc(silu_done, 1)

                def hidden_hi(step):
                    act.wait_ge(hidden_ready, step + 1)
                    nc.scalar.activation(hid_hi[:, :, :].rearrange("p k n -> p (k n)"), hidden, ACT.Copy)\
                        .then_inc(hid_hi_ready, 1)

                def step(t, j, n, last=False):
                    after_gate(t, j, n)
                    split(t, j + 3)
                    if not last:
                        split(t, j + 4)
                    act.wait_ge(chunk_done, 3 * t + (j + 3))
                    hidden_hi(n)
                    if not last:
                        split(t, j + 5)

                after_gate(t, j, FT * f, first=True)
                split(t, j + 3)
                split(t, j + 4)
                hidden_hi(FT * f)
                after_gate(t, j + 2, FT * f + 1)
                split(t, j + 5)
                split(t, j + 6)
                act.wait_ge(chunk_done, 3 * t + (j + 5))
                hidden_hi(FT * f + 1)
                split(t, j + 7)
                with act.Fori(0, FT - 2 - (1 if final else 0)) as i:
                    step(t + i, j + 5, FT * f + i + 2)
                if final:
                    step(t + (FT - 3), j + 5, FT * f + (FT - 1), last=True)

            act.wait_ge(common_landed, 32)
            nc.scalar.activation(c_act[:, :], cp[:, C_COL:C_COL + KT], ACT.Silu).then_inc(c_act_ready, 1)
            act.wait_ge(x_landed, 16)
            for j in range(4):
                squares(0, j, lambda j: None)
            for j in range(SLOTS):
                split(0, j, first=True)
            norm(0, lambda k: cp[:, LNI_B + k:LNI_B + k + 1], True)

            with act.Fori(0, DEPTH) as l:
                t = LT * l

                def evacuate(j):
                    act.wait_ge(chunk_done, 3 * t + (j + 1))
                    bank = B[j % 2][:, :].rearrange("p (m n) -> p m n", m=2)
                    half = 0 if j in (V0, U0, Q0, K0) else 1
                    if j in (V0, V1, U0, U1):
                        out = (v_s if j in (V0, V1) else u_s)[:, :, half * S:(half + 1) * S]
                    else:
                        out = (qT if j in (Q0, Q1) else kT)[:, 2 * half:2 * half + 2, :]
                    scale = HD ** -0.5 if j in (Q0, Q1) else 1.0
                    nc.scalar.activation(out, bank, ACT.Copy, scale=scale).then_inc(proj_evac, 1)
                    split(t, j + 3)

                def exps(h):
                    if h >= 1:
                        act.wait_ge(a_ready, 16 * l + 2 * h)
                    for c in range(2):
                        act.wait_ge(neg_max_ready, 16 * l + (2 * h + c + 1))
                        for m in range(2):
                            last = nc.scalar.activation(probs[:, m, c, :], B[2 + c][:, m * S:(m + 1) * S], ACT.Exp,
                                                        bias=neg_max[:, c, m:m + 1],
                                                        accum_out=sums[:, m, c:c + 1])
                        last.then_inc(probs_ready, 1)

                def keep_P(g):
                    act.wait_ge(P_done, 4 * l + (g + 1))
                    if g >= 1:
                        act.wait_ge(f_done, 4 * l + g)
                    nc.scalar.activation(P_s, B[7][:, :], ACT.Copy).then_inc(P_ready, 1)

                def mix_fourier(g):
                    act.wait_ge(y_done, 4 * l + (g + 1))
                    nc.scalar.activation(mix_hi[:, 4 + g, :], B[1][:, 0:S], ACT.Identity,
                                         bias=lp[:, B_F + g:B_F + g + 1]).then_inc(mix_f_hi, 1)

                evacuate(V0)
                act.wait_ge(full_ready, 16 * l + 8)
                act.wait_ge(x_ready, 16 * l + 8)
                act.dma_start(lp[:, :], layer_params[bass.ds(l, 1)].rearrange("a p n -> (a p) n"))\
                   .then_inc(params_landed, 16)
                act.dma_start(wf[:, :, :], w_f[bass.ds(l, 1)].rearrange("a g c d -> c (a g) d"))\
                   .then_inc(wf_landed, 16)
                for j in (V1, Q0, K0):
                    evacuate(j)
                act.wait_ge(params_landed, 16 * l + 16)
                act.wait_ge(lam_step, 2 * l + 2)
                nc.scalar.activation(lam_exp, lam_sum, ACT.Exp).then_inc(lam_exp_ready, 1)
                for s in range(9):
                    if s >= 1:
                        exps(s - 1)
                    if s < 8 and s % 2 == 1:
                        evacuate(Q1 + s // 2)
                keep_P(0)
                keep_P(1)
                act.wait_ge(o_done, 8 * l + 8)
                for m in range(2):
                    last = nc.scalar.activation(on_s[:, m, :], B[4 + m][:, :], ACT.Square)
                last.then_inc(osq_done, 1)
                keep_P(2)
                act.wait_ge(head_step, 3 * l + 2)
                nc.scalar.activation(head_std, head_var, ACT.Sqrt).then_inc(head_std_ready, 1)
                mix_fourier(0)
                keep_P(3)
                for g in range(1, 4):
                    mix_fourier(g)
                for m in range(2):
                    act.wait_ge(onT_done, 2 * l + (m + 1))
                    nc.scalar.activation(mix_hi[:, 0:4, m * P:(m + 1) * P],
                                         B[2 + m][:, :].rearrange("p (e n) -> p e n", e=4), ACT.Copy,
                                         scale=subg).then_inc(mix_a_hi, 1)
                for j in range(4):
                    squares(2 * l + 1, j, after_residual(2 * l))
                    if j < 3:
                        split(t, O0 + j + 3)
                norm(2 * l + 1, lambda k: lp[:, LN1_B + k:LN1_B + k + 1], True)
                split(t, O0 + 6)
                ffn(t, G0, l)
                for j in range(4):
                    squares(2 * l + 2, j, after_residual(2 * l + 1))
                norm(2 * l + 2, lambda k: lp[:, LN2_B + k:LN2_B + k + 1], True)
                split(t, LAYER_CHUNKS + 2)

            act.wait_ge(x_ready, 8 * 5)
            act.wait_ge(full_ready, 8 * 5)
            for j in range(4):
                squares(5, j, lambda j: None)
            act.wait_ge(mods_step, 6)
            norm(5, lambda k: mods[:, k:k + 1], False)
            ffn(FFN1_T, 0, 2)
            for j in range(4):
                squares(6, j, after_residual(4))
            norm(6, lambda k: mods[:, 24 + k:25 + k], False)
            t = MIX_T
            split(t, 2)
            for j in range(6):
                act.wait_ge(chunk_done, 3 * t + j + 1)
                bank = B[j % 2][:, :].rearrange("p (m n) -> p m n", m=2)
                if j < 2:
                    out, scale = v_s[:, :, j * S:(j + 1) * S], 1.0
                elif j % 2 == 0:
                    out, scale = qT[:, j - 2:j, :], VD ** -0.5
                else:
                    out, scale = kT[:, j - 3:j - 1, :], 1.0
                nc.scalar.activation(out, bank, ACT.Copy, scale=scale).then_inc(proj_evac, 1)
                split(t, j + 3)

            def log1p_exp(h):
                act.wait_ge(z_done, h + 1)
                if h >= 2:
                    act.wait_ge(z_read, h - 1)
                buf = remain[:, h % 2, :]
                nc.scalar.activation(buf, B[2 + h % 2][:, 0:384], ACT.Abs).then_inc(soft_step, 1)
                act.wait_ge(soft_step, 3 * h + 1)
                nc.scalar.activation(buf, buf, ACT.Exp, scale=-1.0).then_inc(soft_step, 1)
                act.wait_ge(soft_step, 3 * h + 2)
                nc.scalar.activation(buf, buf, ACT.Ln, bias=1.0).then_inc(soft_step, 1)

            def exp_a(h):
                act.wait_ge(log_a_ready, h + 1)
                nc.scalar.activation(log_a[:, h % 2, :], log_a[:, h % 2, :], ACT.Exp).then_inc(a_exp_ready, 1)

            def heads_hi(p):
                act.wait_ge(o2_done, 2 * p + 2)
                nc.scalar.activation(mix_hi[:, p, :], B[6 + p % 2][:, 0:S], ACT.Copy).then_inc(o2_hi, 1)

            def conv_round(n):
                act.wait_ge(conv_step, 4 * n + 4)
                nc.scalar.activation(mix_hi[:, 4 + n, :], conv_y[:, n, :], ACT.Copy).then_inc(conv_hi, 1)

            for s in range(12):
                if 1 <= s <= HEADS:
                    log1p_exp(s - 1)
                if 2 <= s < HEADS + 2:
                    exp_a(s - 2)
                if s >= 4 and s % 2 == 0 and s // 2 - 2 < 4:
                    heads_hi(s // 2 - 2)
                if s % 2 == 1:
                    j = 6 + s // 2
                    if j < 10:
                        act.wait_ge(chunk_done, 3 * t + j + 1)
                        out = (gate_b if j < 8 else gate_c)[:, 2 * (j % 2):2 * (j % 2) + 2, :]
                        nc.scalar.activation(out, B[j % 2][:, :].rearrange("p (m n) -> p m n", m=2), ACT.Copy)\
                            .then_inc(proj_evac, 1)
                    split(t, j + 3)
            for n in range(4):
                conv_round(n)
            for j in range(12, 20):
                act.wait_ge(chunk_done, 3 * t + j + 1)
                for n in range(2):
                    tile = 2 * (j % 4) + n
                    which = (j - 12) // 4
                    last = nc.scalar.activation((sig_a, sig_b)[which][:, tile, :], B[j % 2][:, n * S:(n + 1) * S],
                                                ACT.Sigmoid,
                                                bias=cp[:, B_MERGE + 8 * which + tile:B_MERGE + 8 * which + tile + 1])
                last.then_inc(proj_evac, 1)
                split(t, j + 3)
            for j in range(20, 22):
                split(t, j + 3)
            for j in range(22, 24):
                for q in range(2):
                    p = 2 * (j - 22) + q
                    act.wait_ge(merged_done, p + 1)
                    nc.scalar.activation(x_hi[:, 2 * p:2 * p + 2, :], branch[:, 2 * p:2 * p + 2, :], ACT.Copy)\
                        .then_inc(merged_hi, 1)
                split(t, j + 3)
            for j in range(4):
                squares(7, j, after_residual(5))
                if j < 3:
                    split(t, 24 + j + 3)
            norm(7, lambda k: mods[:, 48 + k:49 + k], False)
            split(t, 30)
            ffn(MIX_T, MIX_CHUNKS, 3, final=True)
            for j in range(4):
                squares(8, j, after_residual(6))
            act.wait_ge(var_ready, 9)
            nc.scalar.activation(rstd[:, :], var[:, :], ACT.Sqrt).then_inc(std_ready, 1)

        @block.vector
        def _(dve):
            def split(t, j):
                dve.wait_ge(hi_ready, 3 * t + (j + 1))
                nc.vector.tensor_tensor(w_lo[j % SLOTS][:, :], raw[j % SLOTS][:, :],
                                        w_hi[j % SLOTS][:, :].bitcast(F32), ALU.subtract).then_inc(lo_ready, 1)

            def norm_stats(n, eps, rms):
                dve.wait_ge(stats_done, n + 1)
                if rms:
                    nc.vector.tensor_scalar(var[:, :], STATS[:, S:2 * S], eps, None, ALU.add).then_inc(var_ready, 1)
                else:
                    nc.vector.tensor_copy(mean[:, :], STATS[:, 0:S]).then_inc(mean_ready, 1)
                    dve.wait_ge(mean_ready, n + 1)
                    nc.vector.scalar_tensor_tensor(var[:, :], mean[:, :], -1.0, mean[:, :], ALU.mult, ALU.mult)\
                        .then_inc(mean2_ready, 1)
                    dve.wait_ge(mean2_ready, n + 1)
                    nc.vector.tensor_tensor(var[:, :], STATS[:, S:2 * S], var[:, :], ALU.add).then_inc(var_raw, 1)
                    dve.wait_ge(var_raw, n + 1)
                    nc.vector.tensor_scalar(var[:, :], var[:, :], 0.0, eps, ALU.max, ALU.add).then_inc(var_ready, 1)

            def norm(n, gain, shift, rms):
                norm_stats(n, RMS_EPS if rms else LN_EPS, rms)

                def center(k):
                    nc.vector.tensor_tensor(state[:, k, 1, :], state[:, k, 0, :], mean[:, :], ALU.subtract)\
                        .then_inc(centered, 1)

                if not rms:
                    center(0)
                    center(1)
                dve.wait_ge(std_ready, n + 1)
                nc.vector.reciprocal(rstd[:, :], rstd[:, :]).then_inc(rstd_ready, 1)
                dve.wait_ge(rstd_ready, n + 1)
                for k in range(KT + 1):
                    if k < KT:
                        if not rms:
                            dve.wait_ge(centered, 8 * n + (k + 1))
                        nc.vector.scalar_tensor_tensor(state[:, k, 1, :], state[:, k, 0 if rms else 1, :], gain(k),
                                                       rstd[:, :], ALU.mult, ALU.mult).then_inc(scaled, 1)
                        if not rms and k + 2 < KT:
                            center(k + 2)
                    if k >= 1:
                        dve.wait_ge(x_hi_ready, 8 * n + k)
                        nc.vector.scalar_tensor_tensor(x_lo[:, k - 1, :], state[:, k - 1, 1, :], shift(k - 1),
                                                       x_hi[:, k - 1, :].bitcast(F32), ALU.add, ALU.subtract)\
                            .then_inc(x_ready, 1)

            def residual(j, add, ready):
                ready(j)
                bank = RES[j][:, :].rearrange("p (m n) -> p m n", m=2)
                if add is None:
                    last = nc.vector.scalar_tensor_tensor(state[:, 2 * j:2 * j + 2, 0, :],
                                                          state[:, 2 * j:2 * j + 2, 0, :], ALPHA, bank, ALU.mult,
                                                          ALU.add)
                else:
                    for m in range(2):
                        k = 2 * j + m
                        last = nc.vector.scalar_tensor_tensor(state[:, k, 0, :], bank[:, m, :], gates[:, add, k:k + 1],
                                                              state[:, k, 0, :], ALU.mult, ALU.add)
                last.then_inc(resid_done, 1)

            def ffn(t, j, f, with_ada, final=False):
                def after_up(t, j, n, first=False):
                    dve.wait_ge(chunk_done, 3 * t + (j + 2))
                    dve.wait_ge(silu_done, n + 1)
                    if not first:
                        dve.wait_ge(hid_ready, n)
                    nc.vector.tensor_tensor(hidden, gate_act, B[1][:, :], ALU.mult).then_inc(hidden_ready, 1)

                def hidden_lo(n):
                    dve.wait_ge(hidden_ready, n + 1)
                    dve.wait_ge(hid_hi_ready, n + 1)
                    nc.vector.tensor_tensor(hid_lo[:, :, :].rearrange("p k n -> p (k n)"), hidden,
                                            hid_hi[:, :, :].rearrange("p k n -> p (k n)").bitcast(F32), ALU.subtract)\
                        .then_inc(hid_ready, 1)

                def ada_tile(i):
                    a = ADA_STEPS * f + i
                    dve.wait_ge(ada_landed, 16 * a + 16)
                    nc.vector.tensor_scalar(ada_acc[:, :], ada_raw[:, 0, :], c_act[:, 0:1], None, ALU.mult)\
                        .then_inc(ada_step, 1)
                    for k in range(1, KT):
                        dve.wait_ge(ada_step, KT * a + k)
                        nc.vector.scalar_tensor_tensor(ada_acc[:, :], ada_raw[:, k, :], c_act[:, k:k + 1],
                                                       ada_acc[:, :], ALU.mult, ALU.add).then_inc(ada_step, 1)

                def ada_keep(i):
                    a = ADA_STEPS * f + i
                    dve.wait_ge(ada_reduced, a + 1)
                    nc.vector.tensor_copy(mods[:, bass.ds(4 * a, 4)], B[6][:, 0:4]).then_inc(ada_kept, 1)

                def step(t, j, n, i, last=False):
                    split(t, j + 3)
                    if with_ada:
                        ada_tile(i)
                    after_up(t, j, n)
                    if not last:
                        split(t, j + 4)
                    dve.wait_ge(chunk_done, 3 * t + (j + 3))
                    hidden_lo(n)
                    if not last:
                        split(t, j + 5)
                    if with_ada:
                        ada_keep(i)

                split(t, j + 3)
                after_up(t, j, FT * f, first=True)
                split(t, j + 4)
                hidden_lo(FT * f)
                split(t, j + 5)
                after_up(t, j + 2, FT * f + 1)
                split(t, j + 6)
                dve.wait_ge(chunk_done, 3 * t + (j + 5))
                hidden_lo(FT * f + 1)
                split(t, j + 7)
                with dve.Fori(0, FT - 2 - (1 if final else 0)) as i:
                    step(t + i, j + 5, FT * f + i + 2, i)
                if final:
                    step(t + (FT - 3), j + 5, FT * f + (FT - 1), None, last=True)

            def after_down(t, j, f):
                return lambda b: (dve.wait_ge(down_bank, 3 * f + (b + 1)) if b < 3
                                  else dve.wait_ge(chunk_done, 3 * t + (j + 1)))

            dve.wait_ge(consts_landed, 16)
            dve.wait_ge(common_landed, 32)
            dve.wait_ge(c_act_ready, 1)
            dve.wait_ge(x_landed, 16)
            for j in range(SLOTS):
                split(0, j)
            norm(0, lambda k: cp[:, LNI_G + k:LNI_G + k + 1], lambda k: cp[:, LNI_B + k:LNI_B + k + 1], False)

            with dve.Fori(0, DEPTH) as l:
                t = LT * l

                split(t, V0 + 3)
                dve.wait_ge(params_landed, 16 * l + 16)
                rows = lp[:, LAM_ROWS:LAM_ROWS + 4 * HD]
                nc.vector.tensor_tensor(lam_prod[:, :], rows[:, 0:2 * HD], rows[:, 2 * HD:4 * HD], ALU.mult)\
                    .then_inc(lam_step, 1)
                dve.wait_ge(lam_step, 2 * l + 1)
                nc.vector.reduce_sum(lam_sum, lam_prod[:, :].rearrange("p (a n) -> p a n", a=2), AX_X)\
                    .then_inc(lam_step, 1)
                nc.vector.tensor_scalar(subg, lp[:, SUBLN:SUBLN + 1], lp[:, ONE_MINUS_LI:ONE_MINUS_LI + 1], None,
                                        ALU.mult)

                def unit_max(h, c):
                    dve.wait_ge(scores_done, 16 * l + (2 * h + c + 1))
                    nc.vector.reduce_max(row_max[:, c, :], B[2 + c][:, :].rearrange("p (m n) -> p m n", m=2), AX_X)\
                        .then_inc(row_max_done, 1)

                def unit_neg(h, c):
                    dve.wait_ge(row_max_done, 16 * l + (2 * h + c + 1))
                    nc.vector.tensor_scalar(neg_max[:, c, :], row_max[:, c, :], -1.0, None, ALU.mult)\
                        .then_inc(neg_max_ready, 1)

                def unit_combine(h, m):
                    u = 16 * l + (2 * h + m)
                    dve.wait_ge(probs_ready, 16 * l + (2 * h + 2))
                    nc.vector.reciprocal(inv_sums[:, m, :], sums[:, m, :]).then_inc(inv_ready, 1)
                    dve.wait_ge(inv_ready, u + 1)
                    nc.vector.tensor_scalar(probs[:, m, 1, :], probs[:, m, 1, :], inv_sums[:, m, 1:2], lam, ALU.mult,
                                            ALU.mult).then_inc(second_ready, 1)
                    dve.wait_ge(second_ready, u + 1)
                    if h >= 1:
                        dve.wait_ge(aT_done, 8 * l + h)
                    nc.vector.scalar_tensor_tensor(a_s[:, m, :], probs[:, m, 0, :], inv_sums[:, m, 0:1],
                                                   probs[:, m, 1, :], ALU.mult, ALU.subtract).then_inc(a_ready, 1)

                def keep_aT(h):
                    dve.wait_ge(aT_done, 8 * l + (h + 1))
                    if h >= 1:
                        dve.wait_ge(o_done, 8 * l + h)
                    nc.vector.tensor_copy(aT_s[:, :, :].rearrange("p k n -> p (k n)"), B[6][:, :])\
                        .then_inc(aT_ready, 1)

                def keep_f(g):
                    dve.wait_ge(f_done, 4 * l + (g + 1))
                    if g >= 1:
                        dve.wait_ge(y_done, 4 * l + g)
                    nc.vector.tensor_copy(f_s, B[0][:, 0:S]).then_inc(f_ready, 1)

                def mix_fourier(g):
                    dve.wait_ge(mix_f_hi, 4 * l + (g + 1))
                    nc.vector.scalar_tensor_tensor(mix_lo[:, 4 + g, :], B[1][:, 0:S], lp[:, B_F + g:B_F + g + 1],
                                                   mix_hi[:, 4 + g, :].bitcast(F32), ALU.add, ALU.subtract)\
                        .then_inc(mix_f_ready, 1)

                for j in (V1, Q0, K0):
                    split(t, j + 3)
                dve.wait_ge(lam_exp_ready, l + 1)
                nc.vector.tensor_scalar(lam, lam_exp[:, 0:1], lam_exp[:, 1:2], lp[:, LAM_INIT:LAM_INIT + 1],
                                        ALU.subtract, ALU.add)
                for s in range(9):
                    if s >= 1:
                        unit_max(s - 1, 0)
                        unit_max(s - 1, 1)
                        unit_neg(s - 1, 0)
                        unit_neg(s - 1, 1)
                    if s >= 2:
                        keep_aT(s - 2)
                    if s >= 1:
                        unit_combine(s - 1, 0)
                        unit_combine(s - 1, 1)
                    if s < 8 and s % 2 == 1:
                        split(t, Q1 + s // 2 + 3)
                keep_aT(7)
                keep_f(0)
                dve.wait_ge(osq_done, l + 1)
                nc.vector.reduce_sum(head_ms, on_s[:, :, :].rearrange("p m (h n) -> p (m h) n", n=VD), AX_X)\
                    .then_inc(head_step, 1)
                dve.wait_ge(head_step, 3 * l + 1)
                nc.vector.tensor_scalar(head_var, head_ms, 1.0 / VD, SUBLN_EPS, ALU.mult, ALU.add)\
                    .then_inc(head_step, 1)
                dve.wait_ge(head_std_ready, l + 1)
                nc.vector.reciprocal(head_rstd, head_std).then_inc(head_step, 1)
                dve.wait_ge(head_step, 3 * l + 3)
                for m in range(2):
                    nc.vector.tensor_tensor(on_s[:, m, :].rearrange("p (h n) -> p h n", n=VD),
                                            B[4 + m][:, :].rearrange("p (h n) -> p h n", n=VD),
                                            head_rstd[:, 8 * m:8 * m + 8].unsqueeze(2).broadcast_to([P, 8, VD]),
                                            ALU.mult).then_inc(on_ready, 1)
                keep_f(1)
                mix_fourier(0)
                keep_f(2)
                mix_fourier(1)
                keep_f(3)
                mix_fourier(2)
                mix_fourier(3)
                for m in range(2):
                    dve.wait_ge(mix_a_hi, 2 * l + (m + 1))
                    out = mix_lo[:, 0:4, m * P:(m + 1) * P]
                    nc.vector.scalar_tensor_tensor(out, B[2 + m][:, :].rearrange("p (e n) -> p e n", e=4), subg,
                                                   mix_hi[:, 0:4, m * P:(m + 1) * P].bitcast(F32), ALU.mult,
                                                   ALU.subtract).then_inc(mix_a_ready, 1)
                dve.wait_ge(full_ready, 16 * l + 8)
                for j in range(4):
                    residual(j, None, lambda j: dve.wait_ge(chunk_done, 3 * t + (O0 + j + 1)))
                    if j < 3:
                        split(t, O0 + j + 3)
                norm(2 * l + 1, lambda k: lp[:, LN1_G + k:LN1_G + k + 1], lambda k: lp[:, LN1_B + k:LN1_B + k + 1],
                     False)
                split(t, O0 + 6)
                ffn(t, G0, l, True)
                dve.wait_ge(full_ready, 16 * l + 16)
                for j in range(4):
                    residual(j, None, after_down(t, LAYER_CHUNKS - 1, l))
                norm(2 * l + 2, lambda k: lp[:, LN2_G + k:LN2_G + k + 1], lambda k: lp[:, LN2_B + k:LN2_B + k + 1],
                     False)
                split(t, LAYER_CHUNKS + 2)

            dve.wait_ge(ada_kept, ADA_TILES)
            nc.vector.tensor_tensor(mods[:, :], mods[:, :], cp[:, B_ADA:B_ADA + 72], ALU.add).then_inc(mods_step, 1)
            dve.wait_ge(mods_step, 1)
            for i in range(3):
                nc.vector.scalar_tensor_tensor(gains[:, i, :], mods[:, 24 * i + 8:24 * i + 16], 1.0,
                                               cp[:, NORM_G + 8 * i:NORM_G + 8 * i + 8], ALU.add, ALU.mult)\
                    .then_inc(mods_step, 1)
            modv = mods[:, :].rearrange("p (i m k) -> p i m k", i=3, m=3)
            nc.vector.tensor_scalar(gates[:, 0:3:2, :], modv[:, 0:3:2, 2, :], 0.5, None, ALU.mult)\
                .then_inc(mods_step, 1)
            nc.vector.tensor_copy(gates[:, 1, :], modv[:, 1, 2, :]).then_inc(mods_step, 1)
            dve.wait_ge(mods_step, 6)

            def modulated_norm(n, i):
                norm(n, lambda k: gains[:, i, k:k + 1], lambda k: mods[:, 24 * i + k:24 * i + k + 1], True)

            dve.wait_ge(full_ready, 8 * 5)
            modulated_norm(5, 0)
            ffn(FFN1_T, 0, 2, False)
            for j in range(4):
                residual(j, 0, after_down(FFN1_T, 3 * FT - 1, 2))
            modulated_norm(6, 1)

            t = MIX_T
            split(t, 2)
            nc.vector.memset(vpad[:, :, 0:2], 0.0).then_inc(pads_ready, 1)
            for j in range(6):
                split(t, j + 3)

            def softplus(h):
                dve.wait_ge(soft_step, 3 * h + 3)
                if h >= 2:
                    dve.wait_ge(rem_done, h - 1)
                z, small_log = B[2 + h % 2][:, 0:384], remain[:, h % 2, :]
                nc.vector.scalar_tensor_tensor(soft[:, h % 2, :], z, 0.0, small_log, ALU.max, ALU.add)\
                    .then_inc(soft_raw, 1)
                if h >= 2:
                    dve.wait_ge(o2_done, h - 1)
                nc.vector.scalar_tensor_tensor(log_a[:, h % 2, :], z, 0.0, small_log, ALU.min, ALU.subtract)\
                    .then_inc(z_read, 1)
                dve.wait_ge(soft_raw, h + 1)
                nc.vector.tensor_tensor(soft[:, h % 2, :], soft[:, h % 2, :], mask, ALU.mult)\
                    .then_inc(masked_ready, 1)

            def subtract_remainder(h):
                dve.wait_ge(rem_done, h + 1)
                dve.wait_ge(z_read, h + 1)
                nc.vector.tensor_tensor(log_a[:, h % 2, :], log_a[:, h % 2, :], B[4 + h % 2][:, 0:384],
                                        ALU.subtract).then_inc(log_a_ready, 1)

            def mask_a(h):
                dve.wait_ge(a_exp_ready, h + 1)
                nc.vector.tensor_tensor(log_a[:, h % 2, :], log_a[:, h % 2, :], mask, ALU.mult).then_inc(a2_ready, 1)

            def heads_lo(p):
                dve.wait_ge(o2_hi, p + 1)
                nc.vector.tensor_tensor(mix_lo[:, p, :], B[6 + p % 2][:, 0:S], mix_hi[:, p, :].bitcast(F32),
                                        ALU.subtract).then_inc(o2_ready, 1)

            def conv(i):
                dve.wait_ge(chunk_done, 3 * t + 11 + i)
                dve.wait_ge(proj_evac, 8 * DEPTH + 10)
                nc.vector.tensor_tensor(vpad[:, 2 * i:2 * i + 2, 2:S + 2],
                                        B[i][:, :].rearrange("p (m n) -> p m n", m=2), gate_c[:, 2 * i:2 * i + 2, :],
                                        ALU.mult).then_inc(cx_evac, 1)
                dve.wait_ge(cx_evac, i + 1)
                dve.wait_ge(pads_ready, 1)
                for n in (2 * i, 2 * i + 1):
                    y = conv_y[:, n, :]
                    tap = [cp[:, CONV_W + 4 * w + n:CONV_W + 4 * w + n + 1] for w in range(3)]
                    nc.vector.tensor_scalar(y, vpad[:, n, 0:S], tap[0], None, ALU.mult).then_inc(conv_step, 1)
                    for w in (1, 2):
                        dve.wait_ge(conv_step, 4 * n + w)
                        nc.vector.scalar_tensor_tensor(y, vpad[:, n, w:w + S], tap[w], y, ALU.mult, ALU.add)\
                            .then_inc(conv_step, 1)
                    dve.wait_ge(conv_step, 4 * n + 3)
                    nc.vector.tensor_tensor(y, y, gate_b[:, n, :], ALU.mult).then_inc(conv_step, 1)

            for s in range(12):
                if 2 <= s < HEADS + 2:
                    subtract_remainder(s - 2)
                if 1 <= s <= HEADS:
                    softplus(s - 1)
                if 2 <= s < HEADS + 2:
                    mask_a(s - 2)
                if s >= 4 and s % 2 == 0 and s // 2 - 2 < 4:
                    heads_lo(s // 2 - 2)
                if s % 2 == 1:
                    j = 6 + s // 2
                    if j >= 10:
                        conv(j - 10)
                    split(t, j + 3)
            for n in range(4):
                dve.wait_ge(conv_hi, n + 1)
                nc.vector.tensor_tensor(mix_lo[:, 4 + n, :], conv_y[:, n, :], mix_hi[:, 4 + n, :].bitcast(F32),
                                        ALU.subtract).then_inc(conv_ready, 1)
            for j in range(12, 20):
                split(t, j + 3)
            for j, banks in ((20, B[2:4]), (21, B[4:6])):
                dve.wait_ge(chunk_done, 3 * t + j + 1)
                dve.wait_ge(proj_evac, 8 * DEPTH + 18)
                for q in range(2):
                    p = 2 * (j - 20) + q
                    nc.vector.tensor_tensor(branch[:, 2 * p:2 * p + 2, :],
                                            banks[q][:, :].rearrange("p (m n) -> p m n", m=2),
                                            sig_a[:, 2 * p:2 * p + 2, :], ALU.mult).then_inc(branch_a, 1)
                split(t, j + 3)
            for j, banks in ((22, B[6:8]), (23, B[0:2])):
                dve.wait_ge(chunk_done, 3 * t + j + 1)
                for q in range(2):
                    p = 2 * (j - 22) + q
                    nc.vector.tensor_tensor(sig_b[:, 2 * p:2 * p + 2, :],
                                            banks[q][:, :].rearrange("p (m n) -> p m n", m=2),
                                            sig_b[:, 2 * p:2 * p + 2, :], ALU.mult).then_inc(branch_b, 1)
                for q in range(2):
                    p = 2 * (j - 22) + q
                    dve.wait_ge(branch_a, p + 1)
                    dve.wait_ge(branch_b, p + 1)
                    nc.vector.tensor_tensor(branch[:, 2 * p:2 * p + 2, :], branch[:, 2 * p:2 * p + 2, :],
                                            sig_b[:, 2 * p:2 * p + 2, :], ALU.add).then_inc(merged_done, 1)
                for q in range(2):
                    p = 2 * (j - 22) + q
                    dve.wait_ge(merged_done, p + 1)
                    dve.wait_ge(merged_hi, p + 1)
                    nc.vector.tensor_tensor(x_lo[:, 2 * p:2 * p + 2, :], branch[:, 2 * p:2 * p + 2, :],
                                            x_hi[:, 2 * p:2 * p + 2, :].bitcast(F32), ALU.subtract)\
                        .then_inc(merged_ready, 1)
                split(t, j + 3)
            for j in range(4):
                residual(j, 1, lambda j: dve.wait_ge(chunk_done, 3 * t + 25 + j))
                if j < 3:
                    split(t, 24 + j + 3)
            modulated_norm(7, 2)
            split(t, 30)
            ffn(MIX_T, MIX_CHUNKS, 3, False, final=True)
            for j in range(4):
                residual(j, 2, after_down(MIX_T, MIX_CHUNKS + 3 * FT - 1, 3))

            norm_stats(8, RMS_EPS, True)
            dve.wait_ge(std_ready, 9)
            nc.vector.reciprocal(rstd[:, :], rstd[:, :]).then_inc(rstd_ready, 1)
            dve.wait_ge(rstd_ready, 9)
            for k in range(KT):
                nc.vector.scalar_tensor_tensor(state[:, k, 1, :], state[:, k, 0, :],
                                               cp[:, FINAL_G + k:FINAL_G + k + 1], rstd[:, :], ALU.mult,
                                               ALU.mult).then_inc(out_ready, 1)


def _tiles(w, kt, cols):
    k, n = w.shape
    a = w.reshape(k // (kt * P), kt, P, n // cols, cols)
    return a.transpose(0, 3, 2, 1, 4).reshape(-1, P, kt * cols)


def _ffn_chunks(w_gu, w_down):
    gate, up, down = _tiles(w_gu[:, :FF], KT, 256), _tiles(w_gu[:, FF:], KT, 256), _tiles(w_down, 2, D)
    order = [gate[0], up[0], gate[1], up[1], down[0]]
    for i in range(2, FT):
        order += [gate[i], up[i], down[i - 1]]
    return order + [down[FT - 1]]


def _columns(v):
    return np.asarray(v).reshape(-1, P).T


def _consts():
    i = np.arange(P)
    c32 = np.zeros((P, CONST_COLS), np.float32)
    c32[:, IDENT:IDENT + P] = np.eye(P)
    c32[:, ONES_D:ONES_D + P] = 1.0 / D
    c32[:, TRI:TRI + P] = i[:, None] > i[None, :]
    c32[:, ONES:ONES + P] = 1.0
    valid = i[:, None] < i[None, :]
    c32[:, MASK:MASK + P] = valid
    c32[:, MASK + P:MASK + 2 * P] = 1.0
    c32[:, MASK + 2 * P:MASK + 3 * P] = valid
    s = np.arange(S)
    angle = 2 * np.pi * ((s[:, None] * s[None, :]) % S) / S
    table = np.concatenate([np.cos(angle), np.sin(angle)], 1) / math.sqrt(S)
    c32[:, DFT_S:DFT_S + 4 * S] = table.reshape(2, P, 2 * S).transpose(1, 0, 2).reshape(P, 4 * S)
    angle = 2 * np.pi * ((i[:, None] * i[None, :]) % P) / P
    c32[:, DFT_C:DFT_C + P] = np.cos(angle) / math.sqrt(P)
    c32[:, DFT_C + P:DFT_C + 2 * P] = -np.sin(angle) / math.sqrt(P)
    c16 = np.zeros((P, CONST16_COLS), np.float32)
    for m in range(2):
        c16[:, DIST + m * S:DIST + (m + 1) * S] = np.abs(m * P + i[:, None] - s[None, :])
    for h in range(HEADS):
        c16[:, SLOPES + h * P:SLOPES + (h + 1) * P] = -(2.0 ** (-8.0 * (h + 1) / HEADS)) * np.eye(P)
    return c32, c16


def kernel(**inputs):
    import concourse.bacc as bacc
    import ml_dtypes
    from concourse.bass_utils import run_bass_kernel_spmd

    a = {k: np.asarray(v) for k, v in inputs.items()}
    chunks = []
    for l in range(DEPTH):
        w_in = _tiles(a["w_in"][l], KT, 256)
        q, k, v, u = w_in[0:2], w_in[2:4], w_in[4:6], w_in[6:8]
        chunks += [v[0], v[1], q[0], k[0], q[1], k[1], u[0], u[1]]
        chunks += list(_tiles(a["w_o"][l], KT, 256))
        chunks += _ffn_chunks(a["w_gu"][l], a["w_down"][l])
    chunks += _ffn_chunks(a["ffn1_w_gu_2"][0], a["ffn1_w_down_2"][0])
    m = _tiles(a["w_mix_in_2"][0], KT, 256)
    cb, cc, cx, q, k, v, ga, gb = m[0:2], m[2:4], m[4:6], m[6:8], m[8:10], m[10:12], m[12:16], m[16:20]
    chunks += [v[0], v[1], q[0], k[0], q[1], k[1], *cb, *cc, *cx, *ga, *gb]
    chunks += list(_tiles(a["w_conv_out_2"][0], 4, 512)) + list(_tiles(a["w_attn_out_2"][0], 4, 512))
    chunks += list(_tiles(a["w_out_2"][0], KT, 256))
    chunks += _ffn_chunks(a["ffn2_w_gu_2"][0], a["ffn2_w_down_2"][0])
    stream = np.stack(chunks)
    assert stream.shape == (N_CHUNKS, P, CH)

    layer_params = np.zeros((DEPTH, P, LAYER_COLS), np.float32)
    for l in range(DEPTH):
        lam_init = 0.8 - 0.6 * math.exp(-0.3 * l)
        rows = a["lam_params"][l]
        for at, v in ((LN1_G, a["ln1_g"][l]), (LN1_B, a["ln1_b"][l]), (LN2_G, a["ln2_g"][l]),
                      (LN2_B, a["ln2_b"][l]), (B_F, a["b_f"][l])):
            layer_params[l, :, at:at + v.size // P] = _columns(v)
        layer_params[l, :, SUBLN] = np.concatenate([a["subln_g"][l]] * 2)
        layer_params[l, :, ONE_MINUS_LI] = 1.0 - lam_init
        layer_params[l, :, LAM_INIT] = lam_init
        layer_params[l, :, LAM_ROWS:] = np.concatenate([rows[0], rows[2], rows[1], rows[3]])[None, :]
    common = np.concatenate([_columns(a[n]) for n in (
        "ln_in_g", "ln_in_b", "c_2", "b_ada_2", "norm1_g_2", "norm2_g_2", "norm3_g_2", "b_merge_2", "conv_w_2",
        "final_g_2")], 1)
    assert common.shape == (P, COMMON_COLS)
    consts32, consts16 = _consts()
    arrays = {
        "xT": a["x"][0].T,
        "stream": stream,
        "ada": a["w_ada_2"][0].reshape(KT, P, ADA_TILES, 512).transpose(2, 1, 0, 3),
        "w_f": a["w_f"],
        "layer_params": layer_params,
        "common_params": common,
        "consts32": consts32,
        "consts16": consts16.astype(ml_dtypes.bfloat16),
    }
    arrays = {k: np.ascontiguousarray(v) for k, v in arrays.items()}
    nc = bacc.Bacc("TRN2", target_bir_lowering=False, num_devices=1)
    ins = [nc.dram_tensor(k, v.shape, mybir.dt.from_np(v.dtype), kind="ExternalInput").ap() for k, v in arrays.items()]
    outT = nc.dram_tensor("outT", (D, S), F32, kind="ExternalOutput").ap()
    fused_blocks(nc, *ins, outT)
    r = run_bass_kernel_spmd(nc, [arrays], core_ids=[0])
    return np.ascontiguousarray(r.results[0]["outT"].T)[None]
```

```python
import math
from contextlib import ExitStack

import numpy as np

import concourse.bass as bass
from concourse import mybir

F32 = mybir.dt.float32
F32R = mybir.dt.float32r
BF16 = mybir.dt.bfloat16
ALU = mybir.AluOpType
ACT = mybir.ActivationFunctionType
AX_X = mybir.AxisListType.X

P = 128
S = 256
D = 1024
KT = D // P
DEPTH = 2
HEADS = 8
ATT = 512
HD = 32
VD = 64
GROUPS = 4
FF = 2816
FT = FF // (2 * P)
SLOTS = 3
CH = 2048
LAYER_CHUNKS = 8 + 4 + 3 * FT
MIX_CHUNKS = 20 + 2 + 2 + 4
N_CHUNKS = DEPTH * LAYER_CHUNKS + 2 * 3 * FT + MIX_CHUNKS
ADA_COLS = 384
ADA_TILES = 9 * D // ADA_COLS
ADA_STEPS = FT - 3
MODS = 3 * KT
ALPHA = (2.0 * DEPTH) ** 0.25
LN_EPS = 1e-5
SUBLN_EPS = 1e-5
RMS_EPS = 1e-6

LN1_G, LN1_B, LN2_G, LN2_B, B_F, SUBLN, ONE_MINUS_LI, LAM_INIT, LAM_ROWS = 0, 8, 16, 24, 32, 36, 37, 38, 39
LAYER_COLS = LAM_ROWS + 4 * HD
LNI_G, LNI_B, C_COL, B_ADA, NORM_G, B_MERGE, CONV_W, FINAL_G = 0, 8, 16, 24, 96, 120, 136, 148
COMMON_COLS = FINAL_G + 8
IDENT, ONES_D, TRI, ONES, MASK, DFT_S, DFT_C = 0, 128, 256, 384, 512, 896, 1920
CONST_COLS = DFT_C + 256
DIST, SLOPES = 0, 512
CONST16_COLS = SLOPES + HEADS * P
V0, V1, Q0, K0, Q1, K1, U0, U1, O0, G0 = 0, 1, 2, 3, 4, 5, 6, 7, 8, 12


def fused_blocks(nc, xT, stream, ada, w_f, layer_params, common_params, consts32, consts16, outT):
    with ExitStack() as ctx:
        def sb(name, shape, dt=F32):
            return ctx.enter_context(nc.sbuf_tensor(name, shape, dt))

        def sem(name):
            return ctx.enter_context(nc.semaphore(name))

        raw = [sb(f"raw{i}", [P, CH]) for i in range(SLOTS)]
        w_hi = [sb(f"w_hi{i}", [P, CH], F32R) for i in range(SLOTS)]
        w_lo = [sb(f"w_lo{i}", [P, CH], F32R) for i in range(SLOTS)]
        state = sb("state", [P, KT, 2, S])
        x_hi = sb("x_hi", [P, KT, S], F32R)
        x_lo = sb("x_lo", [P, KT, S], F32R)
        mix_hi = sb("mix_hi", [P, KT, S], F32R)
        mix_lo = sb("mix_lo", [P, KT, S], F32R)
        c32 = sb("c32", [P, CONST_COLS])
        c16 = sb("c16", [P, CONST16_COLS], BF16)
        wf = sb("wf", [P, GROUPS, P])
        lp = sb("lp", [P, LAYER_COLS])
        cp = sb("cp", [P, COMMON_COLS])
        c_act = sb("c_act", [P, KT])
        mods = sb("mods", [P, 72])
        gains = sb("gains", [P, 3, KT])
        gates = sb("gates", [P, 3, KT])
        mean = sb("mean", [P, S])
        var = sb("var", [P, S])
        rstd = sb("rstd", [P, S])
        small = sb("small", [P, 128])
        partial = sb("partial", [P, 2, S])
        partial_last = sb("partial_last", [P, 2, S])
        hid_hi = sb("hid_hi", [P, 2, S], F32R)
        hid_lo = sb("hid_lo", [P, 2, S], F32R)
        hid_hi2 = sb("hid_hi2", [P, 2, S], F32R)
        hid_lo2 = sb("hid_lo2", [P, 2, S], F32R)
        work = sb("work", [P, 14600])

        used = [0]

        def view(n, **dims):
            at = used[0]
            used[0] += n
            assert used[0] <= 14600
            return work[:, at:at + n]

        gate_act = view(2 * S)
        hidden = view(2 * S)
        ffn_end = used[0]
        used[0] = ffn_end
        qT = view(4 * S).rearrange("p (k n) -> p k n", k=4)
        kT = view(4 * S).rearrange("p (k n) -> p k n", k=4)
        v_s = view(2 * ATT).rearrange("p (m n) -> p m n", m=2)
        attn_end = used[0]
        u_s = view(2 * ATT).rearrange("p (m n) -> p m n", m=2)
        probs = view(4 * S).rearrange("p (b c n) -> p b c n", b=2, c=2)
        a_s = view(2 * S).rearrange("p (b n) -> p b n", b=2)
        aT_s = view(2 * S).rearrange("p (k n) -> p k n", k=2)
        P_s = view(2 * S)
        f_s = view(S)
        on_s = view(2 * ATT).rearrange("p (m n) -> p m n", m=2)
        ada_acc = work[:, ffn_end:ffn_end + ADA_STEPS * ADA_COLS]
        ada_raw = view(KT * ADA_COLS).rearrange("p (k n) -> p k n", k=KT)
        lam_prod = view(2 * HD)
        used[0] = attn_end
        gate_b = view(4 * S).rearrange("p (k n) -> p k n", k=4)
        gate_c = view(4 * S).rearrange("p (k n) -> p k n", k=4)
        branch = work[:, attn_end:attn_end + KT * S].rearrange("p (k n) -> p k n", k=KT)
        vpad = view(4 * (S + 2)).rearrange("p (k n) -> p k n", k=4)
        conv_y = view(4 * S).rearrange("p (k n) -> p k n", k=4)
        sig_a = view(KT * S).rearrange("p (k n) -> p k n", k=KT)
        sig_b = view(KT * S).rearrange("p (k n) -> p k n", k=KT)
        remain = work[:, 0:2 * 384].rearrange("p (b n) -> p b n", b=2)
        soft = [view(384), view(384), partial[:, :, :].rearrange("p a n -> p (a n)")[:, 0:384]]
        log_a = view(4 * 384).rearrange("p (b n) -> p b n", b=4)

        ident = c32[:, IDENT:IDENT + P]
        ones_over_d = c32[:, ONES_D:ONES_D + P]
        tri = c32[:, TRI:TRI + P]
        ones = c32[:, ONES:ONES + P]
        mask = c32[:, MASK:MASK + 384]
        dft_s = c32[:, DFT_S:DFT_S + 4 * S].rearrange("p (m n) -> p m n", m=2)
        cos_c = c32[:, DFT_C:DFT_C + P]
        neg_sin_c = c32[:, DFT_C + P:DFT_C + 2 * P]
        neg_max = small[:, 0:4].rearrange("p (c m) -> p c m", c=2)
        sums = small[:, 4:8].rearrange("p (b c) -> p b c", b=2)
        inv_sums = small[:, 8:12].rearrange("p (b c) -> p b c", b=2)
        row_max = small[:, 12:16].rearrange("p (c m) -> p c m", c=2)
        lam_sum, lam_exp, lam, subg = small[:, 16:18], small[:, 18:20], small[:, 20:21], small[:, 21:22]
        head_ms, head_var, head_std, head_rstd = (small[:, a:a + 16] for a in (24, 40, 56, 72))

        B = [ctx.enter_context(nc.psum_tensor(f"bank{i}", [P, 512], F32)) for i in range(8)]
        STATS = B[7]
        SCORES = [B[2], B[3], B[7]]
        RES = [B[4], B[5], B[2], B[3]]

        raw_landed = [sem(f"raw_landed{i}") for i in range(SLOTS)]
        hi_ready = sem("hi_ready")
        lo_ready = sem("lo_ready")
        chunk_done = sem("chunk_done")
        consts_landed = sem("consts_landed")
        common_landed = sem("common_landed")
        mean_weights_landed = sem("mean_weights_landed")
        alibi_landed = sem("alibi_landed")
        x_landed = [sem(f"x_landed{j}") for j in range(4)]
        params_landed = sem("params_landed")
        wf_landed = sem("wf_landed")
        ada_landed = sem("ada_landed")
        ada_step = sem("ada_step")
        ada_reduced = sem("ada_reduced")
        ada_kept = sem("ada_kept")
        c_act_ready = sem("c_act_ready")
        mods_step = sem("mods_step")
        proj_evac = sem("proj_evac")
        resid_done = sem("resid_done")
        squares_done = sem("squares_done")
        partial_done = sem("partial_done")
        stats_done = sem("stats_done")
        mean_ready = sem("mean_ready")
        mean2_ready = sem("mean2_ready")
        var_raw = sem("var_raw")
        var_ready = sem("var_ready")
        std_ready = sem("std_ready")
        rstd_ready = sem("rstd_ready")
        centered = sem("centered")
        scaled = sem("scaled")
        x_hi_ready = sem("x_hi_ready")
        full_ready = sem("full_ready")
        x_ready = sem("x_ready")
        silu_done = sem("silu_done")
        hidden_ready = sem("hidden_ready")
        hid_hi_ready = sem("hid_hi_ready")
        hid_ready = sem("hid_ready")
        down_bank = sem("down_bank")
        scores_done = sem("scores_done")
        row_max_done = sem("row_max_done")
        neg_max_ready = sem("neg_max_ready")
        probs_ready = sem("probs_ready")
        inv_ready = sem("inv_ready")
        second_ready = sem("second_ready")
        a_ready = sem("a_ready")
        aT_done = sem("aT_done")
        aT_ready = sem("aT_ready")
        o_done = sem("o_done")
        lam_step = sem("lam_step")
        lam_exp_ready = sem("lam_exp_ready")
        osq_done = sem("osq_done")
        head_step = sem("head_step")
        head_std_ready = sem("head_std_ready")
        on_ready = sem("on_ready")
        onT_done = sem("onT_done")
        mix_a_hi = sem("mix_a_hi")
        mix_a_ready = sem("mix_a_ready")
        P_done = sem("P_done")
        P_ready = sem("P_ready")
        f_done = sem("f_done")
        f_ready = sem("f_ready")
        y_done = sem("y_done")
        mix_f_hi = sem("mix_f_hi")
        mix_f_ready = sem("mix_f_ready")
        z_done = sem("z_done")
        soft_step = sem("soft_step")
        soft_raw = sem("soft_raw")
        masked_ready = sem("masked_ready")
        z_read = sem("z_read")
        rem_done = sem("rem_done")
        log_a_ready = sem("log_a_ready")
        a_exp_ready = sem("a_exp_ready")
        a2_ready = sem("a2_ready")
        o2_done = sem("o2_done")
        o2_hi = sem("o2_hi")
        o2_ready = sem("o2_ready")
        pads_ready = sem("pads_ready")
        cx_evac = sem("cx_evac")
        conv_step = sem("conv_step")
        conv_hi = sem("conv_hi")
        conv_ready = sem("conv_ready")
        branch_a = sem("branch_a")
        branch_b = sem("branch_b")
        merged_done = sem("merged_done")
        merged_hi = sem("merged_hi")
        merged_ready = sem("merged_ready")
        out_ready = sem("out_ready")
        stored = sem("stored")

        def chunk(tiles, slot, kt):
            return tiles[slot][:, :].rearrange("p (k n) -> p k n", k=kt)

        def landed(t, j):
            return 16 * (t + (j // SLOTS + 1))

        MIX_T = (DEPTH * LAYER_CHUNKS + 3 * FT) // SLOTS
        FFN1_T = DEPTH * LAYER_CHUNKS // SLOTS
        assert LAYER_CHUNKS % SLOTS == 0 and (3 * FT) % SLOTS == 0
        LT = LAYER_CHUNKS // SLOTS

        block = ctx.enter_context(nc.Block())

        @block.sync
        def _(sp):
            for j in range(4):
                sp.dma_start(state[:, 2 * j:2 * j + 2, 0, :],
                             xT[2 * j * P:(2 * j + 2) * P, :].rearrange("(k p) n -> p k n", p=P))\
                  .then_inc(x_landed[j], 16)

            for s in range(SLOTS):
                sp.dma_start(raw[s][:, :], stream[s]).then_inc(raw_landed[s], 16)
                if s == 1:
                    sp.dma_start(c32[:, 0:ONES_D], consts32[:, 0:ONES_D]).then_inc(consts_landed, 16)
                    sp.dma_start(c32[:, TRI:], consts32[:, TRI:]).then_inc(consts_landed, 16)
            with sp.Fori(1, N_CHUNKS // SLOTS) as t:
                for s in range(SLOTS):
                    sp.wait_ge(lo_ready, 3 * t + (s - 2))
                    sp.dma_start(raw[s][:, :], stream[bass.ds(3 * t + s, 1)].rearrange("a p n -> (a p) n"))\
                      .then_inc(raw_landed[s], 16)
            for c in range(N_CHUNKS // SLOTS * SLOTS, N_CHUNKS):
                sp.wait_ge(lo_ready, c - 2)
                sp.dma_start(raw[c % SLOTS][:, :], stream[c]).then_inc(raw_landed[c % SLOTS], 16)
            for j in range(4):
                sp.wait_ge(out_ready, 2 * j + 2)
                sp.dma_start(outT[2 * j * P:(2 * j + 2) * P, :].rearrange("(k p) n -> p k n", p=P),
                             state[:, 2 * j:2 * j + 2, 1, :]).then_inc(stored, 16)
            sp.wait_ge(stored, 64)

        @block.gpsimd
        def _(pool):
            pool.dma_start(cp[:, :], common_params).then_inc(common_landed, 16)
            pool.wait_ge(raw_landed[1], 16)
            pool.dma_start(c16[:, :], consts16).then_inc(alibi_landed, 16)
            pool.dma_start(ada_raw, ada[0]).then_inc(ada_landed, 16)
            with pool.Fori(1, ADA_TILES) as a:
                pool.wait_ge(ada_step, KT * a)
                pool.dma_start(ada_raw, ada[bass.ds(a, 1)].rearrange("a p k n -> (a p) k n")).then_inc(ada_landed, 16)

        @block.tensor
        def _(pe):
            def passes(out, wh, wl, xh, xl, natural, start, stop):
                if natural:
                    pairs = ((xh, wh), (xh, wl), (xl, wh))
                else:
                    pairs = ((wh, xh), (wh, xl), (wl, xh))
                for i, (stationary, moving) in enumerate(pairs):
                    last = nc.tensor.matmul(out, stationary, moving, start=start and i == 0,
                                            stop=stop and i == 2, skip_group_check=True)
                return last

            def projection(t, j, bank, xh, xl, ks=range(KT), order=tuple(range(KT)), natural=False, before=None):
                if ks[0] == 0:
                    pe.wait_ge(lo_ready, 3 * t + (j + 1))
                wh, wl = chunk(w_hi, j % SLOTS, KT), chunk(w_lo, j % SLOTS, KT)
                for i in ks:
                    k = order[i]
                    if before is not None:
                        before(k)
                    for n in range(2):
                        cols = slice(n * P, (n + 1) * P)
                        if natural:
                            last = passes(bank[:, n * S:(n + 1) * S], wh[:, k, :], wl[:, k, :], xh[:, k, cols],
                                          xl[:, k, cols], True, i == 0 and n == 0, i == KT - 1)
                        else:
                            last = passes(bank[:, n * S:(n + 1) * S], wh[:, k, cols], wl[:, k, cols], xh[:, k, :],
                                          xl[:, k, :], False, i == 0 and n == 0, i == KT - 1)
                if ks[-1] == KT - 1:
                    last.then_inc(chunk_done, 1)

            def projection_pair(t, j, banks, xh, xl, before, order=tuple(range(KT)), natural=False):
                pe.wait_ge(lo_ready, 3 * t + (j + 2))
                for i, k in enumerate(order):
                    before(k)
                    for c in range(2):
                        wh, wl = chunk(w_hi, (j + c) % SLOTS, KT), chunk(w_lo, (j + c) % SLOTS, KT)
                        for n in range(2):
                            cols = slice(n * P, (n + 1) * P)
                            out = banks[c][:, n * S:(n + 1) * S]
                            start, stop = i == 0 and n == 0, i == KT - 1
                            if natural:
                                last = passes(out, wh[:, k, :], wl[:, k, :], xh[:, k, cols], xl[:, k, cols], True,
                                              start, stop)
                            else:
                                last = passes(out, wh[:, k, cols], wl[:, k, cols], xh[:, k, :], xl[:, k, :], False,
                                              start, stop)
                        if i == KT - 1:
                            last.then_inc(chunk_done, 1)

            def input_tile(n):
                return lambda k: pe.wait_ge(x_ready, 8 * n + (k + 1))

            def stats(n, rms):
                a = slice(1, 2) if rms else slice(0, 2)
                out = STATS[:, S:2 * S] if rms else STATS[:, :]
                pe.wait_ge(partial_done, 6 * n + 5)
                nc.tensor.matmul(out, ones_over_d, partial[:, a, :].rearrange("p a n -> p (a n)"), start=True,
                                 stop=False)
                pe.wait_ge(partial_done, 6 * n + 6)
                nc.tensor.matmul(out, ones_over_d, partial_last[:, a, :].rearrange("p a n -> p (a n)"), start=False,
                                 stop=True).then_inc(stats_done, 1)

            def ffn_down(t, j, step, first=False, last_step=False, n_out=None, rms=False):
                pe.wait_ge(lo_ready, 3 * t + (j + 1))
                pe.wait_ge(hid_ready, step + 1)
                wh, wl = chunk(w_hi, j % SLOTS, 2), chunk(w_lo, j % SLOTS, 2)
                hh, hl = (hid_hi2, hid_lo2) if last_step else (hid_hi, hid_lo)
                for n in range(KT):
                    cols = slice(n * P, (n + 1) * P)
                    for k in range(2):
                        last = passes(RES[n // 2][:, (n % 2) * S:(n % 2 + 1) * S], wh[:, k, cols], wl[:, k, cols],
                                      hh[:, k, :], hl[:, k, :], False, first and k == 0 and n % 2 == 0,
                                      last_step and k == 1)
                    if last_step and n % 2 == 1 and n < KT - 1:
                        last.then_inc(down_bank, 1)
                last.then_inc(chunk_done, 1)
                if last_step:
                    stats(n_out, rms)

            def ffn(t, j, f, n_in, n_out, rms):
                def gate_up(t, j, i):
                    pe.wait_ge(silu_done, FT * f + i)
                    projection(t, j, B[0], x_hi, x_lo)
                    pe.wait_ge(hidden_ready, FT * f + i)
                    projection(t, j + 1, B[1], x_hi, x_lo)

                projection_pair(t, j, B[0:2], x_hi, x_lo, input_tile(n_in))
                gate_up(t, j + 2, 1)
                ffn_down(t, j + 4, FT * f, first=True)
                with pe.Fori(0, FT - 3) as i:
                    gate_up(t + i, j + 5, i + 2)
                    ffn_down(t + i, j + 7, FT * f + i + 1)
                gate_up(t + (FT - 3), j + 5, FT - 1)
                ffn_down(t + (FT - 3), j + 7, FT * f + (FT - 2))
                ffn_down(t, j + 3 * FT - 1, FT * f + (FT - 1), last_step=True, n_out=n_out, rms=rms)

            def sum_ada(f):
                pe.wait_ge(ada_step, KT * ADA_STEPS * f + KT * ADA_STEPS)
                for q in range(MODS):
                    last = nc.tensor.matmul(B[6][:, q:q + 1], ada_acc[:, q * P:(q + 1) * P], ones[:, 0:1],
                                            start=True, stop=True, skip_group_check=True)
                last.then_inc(ada_reduced, 1)

            pe.wait_ge(mean_weights_landed, 16)
            stats(0, False)

            with pe.Fori(0, DEPTH) as l:
                t = LT * l

                def scores(h):
                    for c in range(2):
                        if 2 * h + c >= 3:
                            pe.wait_ge(probs_ready, 16 * l + (2 * h + c - 2))
                        bank = SCORES[(2 * h + c + 1) % 3]
                        nc.tensor.matmul(bank[:, :], c16[:, SLOPES + h * P:SLOPES + (h + 1) * P],
                                         c16[:, DIST:DIST + 2 * S], start=True, stop=False, skip_group_check=True)
                        r = HD * (2 * (h % 2) + c)
                        for m in range(2):
                            last = nc.tensor.matmul(bank[:, m * S:(m + 1) * S],
                                                    qT[r:r + HD, h // 2, m * P:(m + 1) * P],
                                                    kT[r:r + HD, h // 2, :], start=False, stop=True,
                                                    skip_group_check=True)
                        last.then_inc(scores_done, 1)

                def transpose_a(h):
                    if h >= 1:
                        pe.wait_ge(aT_ready, 8 * l + h)
                    for m in range(2):
                        pe.wait_ge(a_ready, 16 * l + (2 * h + m + 1))
                        for kk in range(2):
                            last = nc.tensor.transpose(B[6][:, kk * S + m * P:kk * S + (m + 1) * P],
                                                       a_s[:, m, kk * P:(kk + 1) * P], ident)
                    last.then_inc(aT_done, 1)

                def values(h):
                    pe.wait_ge(aT_ready, 8 * l + (h + 1))
                    for m in range(2):
                        for kk in range(2):
                            last = nc.tensor.matmul(B[4 + m][:, h * VD:(h + 1) * VD], aT_s[:, kk, m * P:(m + 1) * P],
                                                    v_s[:, kk, h * VD:(h + 1) * VD], start=kk == 0, stop=kk == 1,
                                                    skip_group_check=True)
                    last.then_inc(o_done, 1)

                def fourier_tokens(g):
                    if g >= 1:
                        pe.wait_ge(P_ready, 4 * l + g)
                    else:
                        pe.wait_ge(probs_ready, 16 * l + 14)
                    for m in range(2):
                        last = nc.tensor.matmul(B[7][:, :], u_s[:, m, g * P:(g + 1) * P], dft_s[:, m, :],
                                                start=m == 0, stop=m == 1)
                    last.then_inc(P_done, 1)

                def fourier_features(g):
                    pe.wait_ge(P_ready, 4 * l + (g + 1))
                    if g >= 1:
                        pe.wait_ge(f_ready, 4 * l + g)
                    nc.tensor.matmul(B[0][:, 0:S], cos_c, P_s[:, 0:S], start=True, stop=False)
                    nc.tensor.matmul(B[0][:, 0:S], neg_sin_c, P_s[:, S:2 * S], start=False, stop=True)\
                        .then_inc(f_done, 1)

                def fourier_weights(g):
                    pe.wait_ge(f_ready, 4 * l + (g + 1))
                    if g >= 1:
                        pe.wait_ge(mix_f_ready, 4 * l + g)
                    nc.tensor.matmul(B[1][:, 0:S], wf[:, g, :], f_s, start=True, stop=True).then_inc(y_done, 1)

                def transpose_o(m):
                    pe.wait_ge(on_ready, 2 * l + (m + 1))
                    for e in range(4):
                        last = nc.tensor.transpose(B[2 + m][:, e * P:(e + 1) * P], on_s[:, m, e * P:(e + 1) * P],
                                                   ident)
                    last.then_inc(onT_done, 1)

                projection_pair(t, V0, B[0:2], x_hi, x_lo, lambda k: pe.wait_ge(x_ready, 16 * l + (k + 1)),
                                natural=True)
                for j in (Q0, K0):
                    pe.wait_ge(proj_evac, 8 * l + (j - 1))
                    projection(t, j, B[j % 2], x_hi, x_lo)
                for s in range(8):
                    j = Q1 + s // 2
                    if s >= 2:
                        transpose_a(s - 2)
                    if s % 2 == 0:
                        pe.wait_ge(proj_evac, 8 * l + (j - 1))
                    projection(t, j, B[j % 2], x_hi, x_lo, ks=range(4 * (s % 2), 4 * (s % 2) + 4),
                               natural=j in (U0, U1))
                    if s >= 2:
                        values(s - 2)
                    if s == 0:
                        pe.wait_ge(proj_evac, 8 * l + 4)
                        pe.wait_ge(alibi_landed, 16)
                        pe.wait_ge(consts_landed, 32)
                    if s == 4:
                        pe.wait_ge(proj_evac, 8 * l + 6)
                    scores(s)
                transpose_a(6)
                pe.wait_ge(proj_evac, 8 * l + 8)
                fourier_tokens(0)
                values(6)
                fourier_tokens(1)
                transpose_a(7)
                fourier_features(0)
                values(7)
                fourier_tokens(2)
                fourier_features(1)
                pe.wait_ge(wf_landed, 16 * l + 16)
                fourier_weights(0)
                fourier_tokens(3)
                fourier_features(2)
                fourier_weights(1)
                fourier_features(3)
                fourier_weights(2)
                transpose_o(0)
                fourier_weights(3)
                transpose_o(1)

                def mixed_tile(k):
                    if k >= 4:
                        pe.wait_ge(mix_f_ready, 4 * l + (k - 3))
                    else:
                        pe.wait_ge(mix_a_ready, 2 * l + 2)

                projection_pair(t, O0, RES[0:2], mix_hi, mix_lo, mixed_tile, order=(4, 5, 6, 7, 0, 1, 2, 3))
                for j in (2, 3):
                    projection(t, O0 + j, RES[j], mix_hi, mix_lo)
                stats(2 * l + 1, False)

                ffn(t, G0, l, 2 * l + 1, 2 * l + 2, False)
                sum_ada(l)

            stats(5, True)
            ffn(FFN1_T, 0, 2, 5, 6, True)
            sum_ada(2)

            t = MIX_T
            EV = 8 * DEPTH

            def z_scores(h):
                if h >= 2:
                    pe.wait_ge(z_read, h - 1)
                r = VD * (h % 2)
                q, k = qT[r:r + VD, h // 2, :], kT[r:r + VD, h // 2, :]
                bank = B[2 + h % 2]
                nc.tensor.matmul(bank[:, 0:S], k[:, 0:P], q, start=True, stop=True, skip_group_check=True)
                nc.tensor.matmul(bank[:, S:S + P], k[:, P:S], q[:, P:S], start=False, stop=True,
                                 skip_group_check=True).then_inc(z_done, 1)

            def remainders(h):
                pe.wait_ge(masked_ready, h + 1)
                if h >= 2:
                    pe.wait_ge(log_a_ready, h - 1)
                bank, sp_ = B[4 + h % 2], soft[h % 3]
                nc.tensor.matmul(bank[:, 0:S], tri, sp_[:, 0:S], start=True, stop=False, skip_group_check=True)
                nc.tensor.matmul(bank[:, P:S], ones, sp_[:, S:S + P], start=False, stop=True, skip_group_check=True)
                nc.tensor.matmul(bank[:, S:S + P], tri, sp_[:, S:S + P], start=False, stop=True,
                                 skip_group_check=True).then_inc(rem_done, 1)

            def values2(h):
                pe.wait_ge(a2_ready, h + 1)
                if h % 2 == 0 and h >= 4:
                    pe.wait_ge(o2_ready, h // 2 - 1)
                r = VD * (h % 2)
                out = B[6 + h // 2 % 2][r:r + VD, :]
                nc.tensor.matmul(out[:, 0:S], v_s[:, 0, h * VD:(h + 1) * VD], log_a[:, h % 4, 0:S], start=True,
                                 stop=False, skip_group_check=True)
                nc.tensor.matmul(out[:, P:S], v_s[:, 1, h * VD:(h + 1) * VD], log_a[:, h % 4, S:S + P], start=False,
                                 stop=True, skip_group_check=True).then_inc(o2_done, 1)

            projection_pair(t, 0, B[0:2], x_hi, x_lo, input_tile(6), natural=True)
            for j in range(2, 20):
                if j < 12:
                    pe.wait_ge(proj_evac, EV + j - 1)
                elif 12 <= j < 14:
                    pe.wait_ge(cx_evac, j - 11)
                elif j >= 14:
                    pe.wait_ge(proj_evac, EV + j - 3)
                if j < 6 or j >= 13:
                    projection(t, j, B[j % 2], x_hi, x_lo)
                    continue
                for part in range(2):
                    h = 2 * (j - 6) + part
                    projection(t, j, B[j % 2], x_hi, x_lo, ks=range(4 * part, 4 * part + 4))
                    if h == 0:
                        pe.wait_ge(proj_evac, EV + 6)
                    if 2 <= h < HEADS + 2:
                        remainders(h - 2)
                    if h < HEADS:
                        z_scores(h)
                    if 4 <= h < HEADS + 3:
                        values2(h - 4)
                    if h == HEADS + 4:
                        values2(HEADS - 1)

            def out_projection(j, banks, xh, xl, first_tile, ready):
                pe.wait_ge(lo_ready, 3 * t + (j + 1))
                wh, wl = chunk(w_hi, (j) % SLOTS, 4), chunk(w_lo, (j) % SLOTS, 4)
                for k in range(4):
                    ready(k)
                    for n in range(4):
                        cols = slice(n * P, (n + 1) * P)
                        last = passes(banks[n // 2][:, (n % 2) * S:(n % 2 + 1) * S], wh[:, k, cols], wl[:, k, cols],
                                      xh[:, first_tile + k, :], xl[:, first_tile + k, :], False,
                                      k == 0 and n % 2 == 0, k == 3)
                last.then_inc(chunk_done, 1)

            for j, banks in ((20, B[2:4]), (21, B[4:6])):
                out_projection(j, banks, mix_hi, mix_lo, 4, lambda k: pe.wait_ge(conv_ready, k + 1))
            for j, banks in ((22, B[6:8]), (23, B[0:2])):
                if j == 23:
                    pe.wait_ge(proj_evac, EV + 18)
                out_projection(j, banks, mix_hi, mix_lo, 0, lambda k: pe.wait_ge(o2_ready, k + 1))
            projection_pair(t, 24, RES[0:2], x_hi, x_lo, lambda k: pe.wait_ge(merged_ready, k // 2 + 1))
            for j in (2, 3):
                projection(t, 24 + j, RES[j], x_hi, x_lo)
            stats(7, True)
            ffn(MIX_T, MIX_CHUNKS, 3, 7, 8, True)

        @block.scalar
        def _(act):
            def split(t, j, first=False):
                act.wait_ge(raw_landed[j % SLOTS], landed(t, j))
                if not first:
                    act.wait_ge(chunk_done, 3 * t + (j - 2))
                nc.scalar.activation(w_hi[j % SLOTS][:, :], raw[j % SLOTS][:, :], ACT.Copy).then_inc(hi_ready, 1)

            def squares(n, j, ready):
                ready(j)
                nc.scalar.activation(state[:, 2 * j:2 * j + 2, 1, :], state[:, 2 * j:2 * j + 2, 0, :], ACT.Square)\
                    .then_inc(squares_done, 1)

            def squares_of_pairs(n, m, t, j):
                split(t, j + 3)
                squares(n, 0, after_residual(m))
                squares(n, 1, after_residual(m))
                split(t, j + 4)
                squares(n, 2, after_residual(m))
                split(t, j + 5)
                squares(n, 3, after_residual(m))

            def after_residual(m):
                return lambda j: act.wait_ge(resid_done, 4 * m + (j + 1))

            def norm(n, shift, full):
                act.wait_ge(var_ready, n + 1)
                nc.scalar.activation(rstd[:, :], var[:, :], ACT.Sqrt).then_inc(std_ready, 1)
                for k in range(KT):
                    act.wait_ge(scaled, 8 * n + (k + 1))
                    nc.scalar.activation(x_hi[:, k, :], state[:, k, 1, :], ACT.Identity, bias=shift(k))\
                        .then_inc(x_hi_ready, 1)
                    if full:
                        nc.scalar.activation(state[:, k, 0, :], state[:, k, 1, :], ACT.Identity, bias=shift(k))\
                            .then_inc(full_ready, 1)

            def ffn(t, j, f, final=False):
                def after_gate(t, j, step, first=False):
                    act.wait_ge(chunk_done, 3 * t + (j + 1))
                    if not first:
                        act.wait_ge(hidden_ready, step)
                    nc.scalar.activation(gate_act, B[0][:, :], ACT.Silu).then_inc(silu_done, 1)

                def hidden_hi(step, out=hid_hi):
                    act.wait_ge(hidden_ready, step + 1)
                    nc.scalar.activation(out[:, :, :].rearrange("p k n -> p (k n)"), hidden, ACT.Copy)\
                        .then_inc(hid_hi_ready, 1)

                def step(t, j, n):
                    after_gate(t, j, n)
                    split(t, j + 3)
                    split(t, j + 4)
                    act.wait_ge(chunk_done, 3 * t + (j + 3))
                    hidden_hi(n)
                    split(t, j + 5)

                after_gate(t, j, FT * f, first=True)
                split(t, j + 3)
                split(t, j + 4)
                hidden_hi(FT * f)
                after_gate(t, j + 2, FT * f + 1)
                split(t, j + 5)
                split(t, j + 6)
                act.wait_ge(chunk_done, 3 * t + (j + 5))
                hidden_hi(FT * f + 1)
                split(t, j + 7)
                with act.Fori(0, FT - 3) as i:
                    step(t + i, j + 5, FT * f + i + 2)
                t = t + (FT - 3)
                after_gate(t, j + 5, FT * f + (FT - 1))
                split(t, j + 8)
                hidden_hi(FT * f + (FT - 1), hid_hi2)
                if not final:
                    split(t, j + 9)

            act.dma_start(c32[:, ONES_D:TRI], consts32[:, ONES_D:TRI]).then_inc(mean_weights_landed, 16)
            act.wait_ge(common_landed, 16)
            nc.scalar.activation(c_act[:, :], cp[:, C_COL:C_COL + KT], ACT.Silu).then_inc(c_act_ready, 1)
            for j in range(4):
                squares(0, j, lambda j: act.wait_ge(x_landed[j], 16))
            split(0, 0, first=True)
            split(0, 1, first=True)
            norm(0, lambda k: cp[:, LNI_B + k:LNI_B + k + 1], True)

            with act.Fori(0, DEPTH) as l:
                t = LT * l

                def evacuate(j):
                    act.wait_ge(chunk_done, 3 * t + (j + 1))
                    bank = B[j % 2][:, :].rearrange("p (m n) -> p m n", m=2)
                    half = 0 if j in (V0, U0, Q0, K0) else 1
                    if j in (V0, V1, U0, U1):
                        out = (v_s if j in (V0, V1) else u_s)[:, :, half * S:(half + 1) * S]
                    else:
                        out = (qT if j in (Q0, Q1) else kT)[:, 2 * half:2 * half + 2, :]
                    scale = HD ** -0.5 if j in (Q0, Q1) else 1.0
                    nc.scalar.activation(out, bank, ACT.Copy, scale=scale).then_inc(proj_evac, 1)
                    split(t, j + 3)

                def exps(h):
                    if h >= 1:
                        act.wait_ge(a_ready, 16 * l + 2 * h)
                    for c in range(2):
                        act.wait_ge(neg_max_ready, 16 * l + (2 * h + c + 1))
                        bank = SCORES[(2 * h + c + 1) % 3]
                        for m in range(2):
                            last = nc.scalar.activation(probs[:, m, c, :], bank[:, m * S:(m + 1) * S], ACT.Exp,
                                                        bias=neg_max[:, c, m:m + 1],
                                                        accum_out=sums[:, m, c:c + 1])
                        last.then_inc(probs_ready, 1)

                def keep_P(g):
                    act.wait_ge(P_done, 4 * l + (g + 1))
                    if g >= 1:
                        act.wait_ge(f_done, 4 * l + g)
                    nc.scalar.activation(P_s, B[7][:, :], ACT.Copy).then_inc(P_ready, 1)

                def mix_fourier(g):
                    act.wait_ge(y_done, 4 * l + (g + 1))
                    nc.scalar.activation(mix_hi[:, 4 + g, :], B[1][:, 0:S], ACT.Identity,
                                         bias=lp[:, B_F + g:B_F + g + 1]).then_inc(mix_f_hi, 1)

                split(t, 2, first=True)
                evacuate(V0)
                act.wait_ge(full_ready, 16 * l + 8)
                act.wait_ge(x_ready, 16 * l + 8)
                act.dma_start(lp[:, :], layer_params[bass.ds(l, 1)].rearrange("a p n -> (a p) n"))\
                   .then_inc(params_landed, 16)
                act.dma_start(wf[:, :, :], w_f[bass.ds(l, 1)].rearrange("a g c d -> c (a g) d"))\
                   .then_inc(wf_landed, 16)
                for j in (V1, Q0, K0):
                    evacuate(j)
                act.wait_ge(params_landed, 16 * l + 16)
                act.wait_ge(lam_step, 2 * l + 2)
                nc.scalar.activation(lam_exp, lam_sum, ACT.Exp).then_inc(lam_exp_ready, 1)
                for s in range(9):
                    if s >= 1:
                        exps(s - 1)
                    if s < 8 and s % 2 == 1:
                        evacuate(Q1 + s // 2)
                keep_P(0)
                keep_P(1)
                act.wait_ge(o_done, 8 * l + 8)
                for m in range(2):
                    last = nc.scalar.activation(on_s[:, m, :], B[4 + m][:, :], ACT.Square)
                last.then_inc(osq_done, 1)
                keep_P(2)
                act.wait_ge(head_step, 3 * l + 2)
                nc.scalar.activation(head_std, head_var, ACT.Sqrt).then_inc(head_std_ready, 1)
                mix_fourier(0)
                keep_P(3)
                for g in range(1, 4):
                    mix_fourier(g)
                for m in range(2):
                    act.wait_ge(onT_done, 2 * l + (m + 1))
                    nc.scalar.activation(mix_hi[:, 0:4, m * P:(m + 1) * P],
                                         B[2 + m][:, :].rearrange("p (e n) -> p e n", e=4), ACT.Copy,
                                         scale=subg).then_inc(mix_a_hi, 1)
                squares_of_pairs(2 * l + 1, 2 * l, t, O0)
                norm(2 * l + 1, lambda k: lp[:, LN1_B + k:LN1_B + k + 1], True)
                split(t, O0 + 6)
                ffn(t, G0, l)
                for j in range(4):
                    squares(2 * l + 2, j, after_residual(2 * l + 1))
                split(t, LAYER_CHUNKS + 1)
                norm(2 * l + 2, lambda k: lp[:, LN2_B + k:LN2_B + k + 1], True)

            act.wait_ge(ada_kept, 1)
            for j in range(4):
                act.wait_ge(x_ready, 8 * 4 + 2 * j + 2)
                act.wait_ge(full_ready, 8 * 4 + 2 * j + 2)
                squares(5, j, lambda j: None)
            norm(5, lambda k: mods[:, k:k + 1], False)
            split(FFN1_T, 2)
            ffn(FFN1_T, 0, 2)
            act.wait_ge(ada_kept, 2)
            for j in range(4):
                squares(6, j, after_residual(4))
            split(FFN1_T, 3 * FT + 1)
            norm(6, lambda k: mods[:, 24 + k:25 + k], False)
            t = MIX_T
            split(t, 2)
            for j in range(6):
                act.wait_ge(chunk_done, 3 * t + j + 1)
                bank = B[j % 2][:, :].rearrange("p (m n) -> p m n", m=2)
                if j < 2:
                    out, scale = v_s[:, :, j * S:(j + 1) * S], 1.0
                elif j % 2 == 0:
                    out, scale = qT[:, j - 2:j, :], VD ** -0.5
                else:
                    out, scale = kT[:, j - 3:j - 1, :], 1.0
                nc.scalar.activation(out, bank, ACT.Copy, scale=scale).then_inc(proj_evac, 1)
                split(t, j + 3)

            def log1p_exp(h):
                act.wait_ge(z_done, h + 1)
                if h >= 2:
                    act.wait_ge(z_read, h - 1)
                buf = remain[:, h % 2, :]
                nc.scalar.activation(buf, B[2 + h % 2][:, 0:384], ACT.Abs).then_inc(soft_step, 1)
                act.wait_ge(soft_step, 3 * h + 1)
                nc.scalar.activation(buf, buf, ACT.Exp, scale=-1.0).then_inc(soft_step, 1)
                act.wait_ge(soft_step, 3 * h + 2)
                nc.scalar.activation(buf, buf, ACT.Ln, bias=1.0).then_inc(soft_step, 1)

            def exp_a(h):
                act.wait_ge(log_a_ready, h + 1)
                nc.scalar.activation(log_a[:, h % 4, :], log_a[:, h % 4, :], ACT.Exp).then_inc(a_exp_ready, 1)

            def heads_hi(p):
                act.wait_ge(o2_done, 2 * p + 2)
                nc.scalar.activation(mix_hi[:, p, :], B[6 + p % 2][:, 0:S], ACT.Copy).then_inc(o2_hi, 1)

            def conv_round(n):
                act.wait_ge(conv_step, 4 * n + 4)
                nc.scalar.activation(mix_hi[:, 4 + n, :], conv_y[:, n, :], ACT.Copy).then_inc(conv_hi, 1)

            for s in range(13):
                if 1 <= s <= HEADS:
                    log1p_exp(s - 1)
                if 3 <= s < HEADS + 3:
                    exp_a(s - 3)
                if s >= 6 and s % 2 == 0:
                    heads_hi((s - 6) // 2)
                if s % 2 == 1:
                    split(t, 6 + s // 2 + 3)
            for n in range(4):
                conv_round(n)
            for j in range(12, 20):
                act.wait_ge(chunk_done, 3 * t + j + 1)
                for n in range(2):
                    tile = 2 * (j % 4) + n
                    which = (j - 12) // 4
                    last = nc.scalar.activation((sig_a, sig_b)[which][:, tile, :], B[j % 2][:, n * S:(n + 1) * S],
                                                ACT.Sigmoid,
                                                bias=cp[:, B_MERGE + 8 * which + tile:B_MERGE + 8 * which + tile + 1])
                last.then_inc(proj_evac, 1)
                split(t, j + 3)
            for j in range(20, 22):
                split(t, j + 3)
            for j in range(22, 24):
                if j == 22:
                    split(t, j + 3)
                for q in range(2):
                    p = 2 * (j - 22) + q
                    act.wait_ge(merged_done, p + 1)
                    nc.scalar.activation(x_hi[:, 2 * p:2 * p + 2, :], branch[:, 2 * p:2 * p + 2, :], ACT.Copy)\
                        .then_inc(merged_hi, 1)
                if j == 23:
                    split(t, j + 3)
            act.wait_ge(ada_kept, 3)
            squares_of_pairs(7, 5, t, 24)
            norm(7, lambda k: mods[:, 48 + k:49 + k], False)
            split(t, 30)
            ffn(MIX_T, MIX_CHUNKS, 3, final=True)
            for j in range(4):
                squares(8, j, after_residual(6))
            act.wait_ge(var_ready, 9)
            nc.scalar.activation(rstd[:, :], var[:, :], ACT.Sqrt).then_inc(std_ready, 1)

        @block.vector
        def _(dve):
            def split(t, j):
                dve.wait_ge(hi_ready, 3 * t + (j + 1))
                nc.vector.tensor_tensor(w_lo[j % SLOTS][:, :], raw[j % SLOTS][:, :],
                                        w_hi[j % SLOTS][:, :].bitcast(F32), ALU.subtract).then_inc(lo_ready, 1)

            def norm_stats(n, eps, rms):
                dve.wait_ge(stats_done, n + 1)
                if rms:
                    nc.vector.tensor_scalar(var[:, :], STATS[:, S:2 * S], eps, None, ALU.add).then_inc(var_ready, 1)
                else:
                    nc.vector.tensor_copy(mean[:, :], STATS[:, 0:S]).then_inc(mean_ready, 1)
                    dve.wait_ge(mean_ready, n + 1)
                    nc.vector.scalar_tensor_tensor(var[:, :], mean[:, :], -1.0, mean[:, :], ALU.mult, ALU.mult)\
                        .then_inc(mean2_ready, 1)
                    dve.wait_ge(mean2_ready, n + 1)
                    nc.vector.tensor_tensor(var[:, :], STATS[:, S:2 * S], var[:, :], ALU.add).then_inc(var_raw, 1)
                    dve.wait_ge(var_raw, n + 1)
                    nc.vector.tensor_scalar(var[:, :], var[:, :], 0.0, eps, ALU.max, ALU.add).then_inc(var_ready, 1)

            def norm(n, gain, shift, rms):
                norm_stats(n, RMS_EPS if rms else LN_EPS, rms)

                def center(k):
                    nc.vector.tensor_tensor(state[:, k, 1, :], state[:, k, 0, :], mean[:, :], ALU.subtract)\
                        .then_inc(centered, 1)

                if not rms:
                    center(0)
                    center(1)
                dve.wait_ge(std_ready, n + 1)
                nc.vector.reciprocal(rstd[:, :], rstd[:, :]).then_inc(rstd_ready, 1)
                dve.wait_ge(rstd_ready, n + 1)
                for k in range(KT + 1):
                    if k < KT:
                        if not rms:
                            dve.wait_ge(centered, 8 * n + (k + 1))
                        nc.vector.scalar_tensor_tensor(state[:, k, 1, :], state[:, k, 0 if rms else 1, :], gain(k),
                                                       rstd[:, :], ALU.mult, ALU.mult).then_inc(scaled, 1)
                        if not rms and k + 2 < KT:
                            center(k + 2)
                    if k >= 1:
                        dve.wait_ge(x_hi_ready, 8 * n + k)
                        nc.vector.scalar_tensor_tensor(x_lo[:, k - 1, :], state[:, k - 1, 1, :], shift(k - 1),
                                                       x_hi[:, k - 1, :].bitcast(F32), ALU.add, ALU.subtract)\
                            .then_inc(x_ready, 1)

            def residual(j, add, ready):
                ready(j)
                bank = RES[j][:, :].rearrange("p (m n) -> p m n", m=2)
                if add is None:
                    last = nc.vector.scalar_tensor_tensor(state[:, 2 * j:2 * j + 2, 0, :],
                                                          state[:, 2 * j:2 * j + 2, 0, :], ALPHA, bank, ALU.mult,
                                                          ALU.add)
                else:
                    for m in range(2):
                        k = 2 * j + m
                        last = nc.vector.scalar_tensor_tensor(state[:, k, 0, :], bank[:, m, :], gates[:, add, k:k + 1],
                                                              state[:, k, 0, :], ALU.mult, ALU.add)
                last.then_inc(resid_done, 1)

            def accumulate(n, j, rms):
                a = slice(1, 2) if rms else slice(0, 2)
                dve.wait_ge(squares_done, 4 * n + (j + 1))
                if j == 3:
                    nc.vector.tensor_tensor(partial_last[:, a, :], state[:, 6, a, :], state[:, 7, a, :], ALU.add)\
                        .then_inc(partial_done, 1)
                    return
                for k in (2 * j, 2 * j + 1):
                    if k == 0:
                        continue
                    if k >= 2:
                        dve.wait_ge(partial_done, 6 * n + (k - 1))
                    nc.vector.tensor_tensor(partial[:, a, :], state[:, 0, a, :] if k == 1 else partial[:, a, :],
                                            state[:, k, a, :], ALU.add).then_inc(partial_done, 1)

            def residual_sums(n, add, ready, rms=False):
                for j in range(4):
                    residual(j, add, ready)
                    if j >= 1:
                        accumulate(n, j - 1, rms)
                accumulate(n, 3, rms)

            def residual_sums_of_pairs(n, add, t, j, rms=False):
                ready = lambda b: dve.wait_ge(chunk_done, 3 * t + (j + b + 1))
                residual(0, add, ready)
                residual(1, add, ready)
                split(t, j + 3)
                accumulate(n, 0, rms)
                accumulate(n, 1, rms)
                residual(2, add, ready)
                split(t, j + 4)
                accumulate(n, 2, rms)
                residual(3, add, ready)
                accumulate(n, 3, rms)
                split(t, j + 5)

            def keep_mods(f):
                dve.wait_ge(ada_reduced, f + 1)
                nc.vector.tensor_tensor(mods[:, bass.ds(MODS * f, MODS)], B[6][:, 0:MODS],
                                        cp[:, bass.ds(MODS * f + B_ADA, MODS)], ALU.add).then_inc(ada_kept, 1)

            def ffn(t, j, f, with_ada, final=False):
                def after_up(t, j, n, first=False):
                    dve.wait_ge(chunk_done, 3 * t + (j + 2))
                    dve.wait_ge(silu_done, n + 1)
                    if not first:
                        dve.wait_ge(hid_ready, n)
                    nc.vector.tensor_tensor(hidden, gate_act, B[1][:, :], ALU.mult).then_inc(hidden_ready, 1)

                def hidden_lo(n, hi=hid_hi, lo=hid_lo):
                    dve.wait_ge(hidden_ready, n + 1)
                    dve.wait_ge(hid_hi_ready, n + 1)
                    nc.vector.tensor_tensor(lo[:, :, :].rearrange("p k n -> p (k n)"), hidden,
                                            hi[:, :, :].rearrange("p k n -> p (k n)").bitcast(F32), ALU.subtract)\
                        .then_inc(hid_ready, 1)

                def ada_tile(i):
                    a = ADA_STEPS * f + i
                    acc = ada_acc[:, bass.ds(ADA_COLS * i, ADA_COLS)]
                    dve.wait_ge(ada_landed, 16 * a + 16)
                    nc.vector.tensor_scalar(acc, ada_raw[:, 0, :], c_act[:, 0:1], None, ALU.mult).then_inc(ada_step, 1)
                    for k in range(1, KT):
                        dve.wait_ge(ada_step, KT * a + k)
                        nc.vector.scalar_tensor_tensor(acc, ada_raw[:, k, :], c_act[:, k:k + 1], acc, ALU.mult,
                                                       ALU.add).then_inc(ada_step, 1)

                def step(t, j, n, i):
                    split(t, j + 3)
                    after_up(t, j, n)
                    split(t, j + 4)
                    dve.wait_ge(chunk_done, 3 * t + (j + 3))
                    hidden_lo(n)
                    split(t, j + 5)
                    if with_ada:
                        ada_tile(i)

                split(t, j + 3)
                after_up(t, j, FT * f, first=True)
                split(t, j + 4)
                hidden_lo(FT * f)
                split(t, j + 5)
                after_up(t, j + 2, FT * f + 1)
                split(t, j + 6)
                dve.wait_ge(chunk_done, 3 * t + (j + 5))
                hidden_lo(FT * f + 1)
                split(t, j + 7)
                with dve.Fori(0, FT - 3) as i:
                    step(t + i, j + 5, FT * f + i + 2, i)
                t = t + (FT - 3)
                split(t, j + 8)
                after_up(t, j + 5, FT * f + (FT - 1))
                hidden_lo(FT * f + (FT - 1), hid_hi2, hid_lo2)
                if not final:
                    split(t, j + 9)

            def after_down(t, j, f):
                return lambda b: (dve.wait_ge(down_bank, 3 * f + (b + 1)) if b < 3
                                  else dve.wait_ge(chunk_done, 3 * t + (j + 1)))

            for j in range(4):
                dve.wait_ge(x_landed[j], 16)
                accumulate(0, j, False)
            split(0, 0)
            split(0, 1)
            dve.wait_ge(common_landed, 16)
            norm(0, lambda k: cp[:, LNI_G + k:LNI_G + k + 1], lambda k: cp[:, LNI_B + k:LNI_B + k + 1], False)
            dve.wait_ge(c_act_ready, 1)

            with dve.Fori(0, DEPTH) as l:
                t = LT * l

                split(t, V0 + 2)
                split(t, V0 + 3)
                dve.wait_ge(params_landed, 16 * l + 16)
                rows = lp[:, LAM_ROWS:LAM_ROWS + 4 * HD]
                nc.vector.tensor_tensor(lam_prod, rows[:, 0:2 * HD], rows[:, 2 * HD:4 * HD], ALU.mult)\
                    .then_inc(lam_step, 1)
                dve.wait_ge(lam_step, 2 * l + 1)
                nc.vector.reduce_sum(lam_sum, lam_prod.rearrange("p (a n) -> p a n", a=2), AX_X)\
                    .then_inc(lam_step, 1)
                nc.vector.tensor_scalar(subg, lp[:, SUBLN:SUBLN + 1], lp[:, ONE_MINUS_LI:ONE_MINUS_LI + 1], None,
                                        ALU.mult)

                def unit_max(h, c):
                    dve.wait_ge(scores_done, 16 * l + (2 * h + c + 1))
                    nc.vector.reduce_max(row_max[:, c, :], SCORES[(2 * h + c + 1) % 3][:, :].rearrange("p (m n) -> p m n", m=2), AX_X)\
                        .then_inc(row_max_done, 1)

                def unit_neg(h, c):
                    dve.wait_ge(row_max_done, 16 * l + (2 * h + c + 1))
                    if h >= 1:
                        dve.wait_ge(probs_ready, 16 * l + (2 * h + c - 1))
                    nc.vector.tensor_scalar(neg_max[:, c, :], row_max[:, c, :], -1.0, None, ALU.mult)\
                        .then_inc(neg_max_ready, 1)

                def unit_combine(h, m):
                    u = 16 * l + (2 * h + m)
                    dve.wait_ge(probs_ready, 16 * l + (2 * h + 2))
                    nc.vector.reciprocal(inv_sums[:, m, :], sums[:, m, :]).then_inc(inv_ready, 1)
                    dve.wait_ge(inv_ready, u + 1)
                    nc.vector.tensor_scalar(probs[:, m, 1, :], probs[:, m, 1, :], inv_sums[:, m, 1:2], lam, ALU.mult,
                                            ALU.mult).then_inc(second_ready, 1)
                    dve.wait_ge(second_ready, u + 1)
                    if h >= 1:
                        dve.wait_ge(aT_done, 8 * l + h)
                    nc.vector.scalar_tensor_tensor(a_s[:, m, :], probs[:, m, 0, :], inv_sums[:, m, 0:1],
                                                   probs[:, m, 1, :], ALU.mult, ALU.subtract).then_inc(a_ready, 1)

                def keep_aT(h):
                    dve.wait_ge(aT_done, 8 * l + (h + 1))
                    if h >= 1:
                        dve.wait_ge(o_done, 8 * l + h)
                    nc.vector.tensor_copy(aT_s[:, :, :].rearrange("p k n -> p (k n)"), B[6][:, :])\
                        .then_inc(aT_ready, 1)

                def keep_f(g):
                    dve.wait_ge(f_done, 4 * l + (g + 1))
                    if g >= 1:
                        dve.wait_ge(y_done, 4 * l + g)
                    nc.vector.tensor_copy(f_s, B[0][:, 0:S]).then_inc(f_ready, 1)

                def mix_fourier(g):
                    dve.wait_ge(mix_f_hi, 4 * l + (g + 1))
                    nc.vector.scalar_tensor_tensor(mix_lo[:, 4 + g, :], B[1][:, 0:S], lp[:, B_F + g:B_F + g + 1],
                                                   mix_hi[:, 4 + g, :].bitcast(F32), ALU.add, ALU.subtract)\
                        .then_inc(mix_f_ready, 1)

                for j in (V1, Q0, K0):
                    split(t, j + 3)
                dve.wait_ge(lam_exp_ready, l + 1)
                nc.vector.tensor_scalar(lam, lam_exp[:, 0:1], lam_exp[:, 1:2], lp[:, LAM_INIT:LAM_INIT + 1],
                                        ALU.subtract, ALU.add)
                for s in range(9):
                    if s >= 1:
                        unit_max(s - 1, 0)
                        unit_max(s - 1, 1)
                        unit_neg(s - 1, 0)
                        unit_neg(s - 1, 1)
                    if s >= 2:
                        keep_aT(s - 2)
                    if s >= 1:
                        unit_combine(s - 1, 0)
                        unit_combine(s - 1, 1)
                    if s < 8 and s % 2 == 1:
                        split(t, Q1 + s // 2 + 3)
                keep_aT(7)
                keep_f(0)
                dve.wait_ge(osq_done, l + 1)
                nc.vector.reduce_sum(head_ms, on_s[:, :, :].rearrange("p m (h n) -> p (m h) n", n=VD), AX_X)\
                    .then_inc(head_step, 1)
                dve.wait_ge(head_step, 3 * l + 1)
                nc.vector.tensor_scalar(head_var, head_ms, 1.0 / VD, SUBLN_EPS, ALU.mult, ALU.add)\
                    .then_inc(head_step, 1)
                dve.wait_ge(head_std_ready, l + 1)
                nc.vector.reciprocal(head_rstd, head_std).then_inc(head_step, 1)
                dve.wait_ge(head_step, 3 * l + 3)
                for m in range(2):
                    nc.vector.tensor_tensor(on_s[:, m, :].rearrange("p (h n) -> p h n", n=VD),
                                            B[4 + m][:, :].rearrange("p (h n) -> p h n", n=VD),
                                            head_rstd[:, 8 * m:8 * m + 8].unsqueeze(2).broadcast_to([P, 8, VD]),
                                            ALU.mult).then_inc(on_ready, 1)
                keep_f(1)
                mix_fourier(0)
                keep_f(2)
                mix_fourier(1)
                keep_f(3)
                mix_fourier(2)
                mix_fourier(3)
                for m in range(2):
                    dve.wait_ge(mix_a_hi, 2 * l + (m + 1))
                    out = mix_lo[:, 0:4, m * P:(m + 1) * P]
                    nc.vector.scalar_tensor_tensor(out, B[2 + m][:, :].rearrange("p (e n) -> p e n", e=4), subg,
                                                   mix_hi[:, 0:4, m * P:(m + 1) * P].bitcast(F32), ALU.mult,
                                                   ALU.subtract).then_inc(mix_a_ready, 1)
                dve.wait_ge(full_ready, 16 * l + 8)
                residual_sums_of_pairs(2 * l + 1, None, t, O0)
                norm(2 * l + 1, lambda k: lp[:, LN1_G + k:LN1_G + k + 1], lambda k: lp[:, LN1_B + k:LN1_B + k + 1],
                     False)
                split(t, O0 + 6)
                ffn(t, G0, l, True)
                dve.wait_ge(full_ready, 16 * l + 16)
                residual_sums(2 * l + 2, None, after_down(t, LAYER_CHUNKS - 1, l))
                split(t, LAYER_CHUNKS + 1)
                norm(2 * l + 2, lambda k: lp[:, LN2_G + k:LN2_G + k + 1], lambda k: lp[:, LN2_B + k:LN2_B + k + 1],
                     False)
                keep_mods(l)

            def modulation(i):
                dve.wait_ge(ada_kept, i + 1)
                nc.vector.scalar_tensor_tensor(gains[:, i, :], mods[:, MODS * i + KT:MODS * i + 2 * KT], 1.0,
                                               cp[:, NORM_G + KT * i:NORM_G + KT * i + KT], ALU.add, ALU.mult)\
                    .then_inc(mods_step, 1)
                nc.vector.tensor_scalar(gates[:, i, :], mods[:, MODS * i + 2 * KT:MODS * i + 3 * KT],
                                        1.0 if i == 1 else 0.5, None, ALU.mult).then_inc(mods_step, 1)

            modulation(0)
            modulation(1)

            def modulated_norm(n, i):
                norm(n, lambda k: gains[:, i, k:k + 1], lambda k: mods[:, 24 * i + k:24 * i + k + 1], True)

            dve.wait_ge(full_ready, 8 * 5)
            dve.wait_ge(mods_step, 4)
            for j in range(4):
                accumulate(5, j, True)
            modulated_norm(5, 0)
            split(FFN1_T, 2)
            ffn(FFN1_T, 0, 2, True)
            residual_sums(6, 0, after_down(FFN1_T, 3 * FT - 1, 2), rms=True)
            split(FFN1_T, 3 * FT + 1)
            modulated_norm(6, 1)
            keep_mods(2)
            modulation(2)

            t = MIX_T
            split(t, 2)
            dve.wait_ge(consts_landed, 32)
            nc.vector.memset(vpad[:, :, 0:2], 0.0).then_inc(pads_ready, 1)
            for j in range(6):
                split(t, j + 3)

            def softplus(h):
                dve.wait_ge(soft_step, 3 * h + 3)
                if h >= 3:
                    dve.wait_ge(rem_done, h - 2)
                z, small_log = B[2 + h % 2][:, 0:384], remain[:, h % 2, :]
                nc.vector.scalar_tensor_tensor(soft[h % 3], z, 0.0, small_log, ALU.max, ALU.add)\
                    .then_inc(soft_raw, 1)
                if h >= 4:
                    dve.wait_ge(o2_done, h - 3)
                nc.vector.scalar_tensor_tensor(log_a[:, h % 4, :], z, 0.0, small_log, ALU.min, ALU.subtract)\
                    .then_inc(z_read, 1)
                dve.wait_ge(soft_raw, h + 1)
                nc.vector.tensor_tensor(soft[h % 3], soft[h % 3], mask, ALU.mult)\
                    .then_inc(masked_ready, 1)

            def subtract_remainder(h):
                dve.wait_ge(rem_done, h + 1)
                dve.wait_ge(z_read, h + 1)
                nc.vector.tensor_tensor(log_a[:, h % 4, :], log_a[:, h % 4, :], B[4 + h % 2][:, 0:384],
                                        ALU.subtract).then_inc(log_a_ready, 1)

            def mask_a(h):
                dve.wait_ge(a_exp_ready, h + 1)
                nc.vector.tensor_tensor(log_a[:, h % 4, :], log_a[:, h % 4, :], mask, ALU.mult).then_inc(a2_ready, 1)

            def heads_lo(p):
                dve.wait_ge(o2_hi, p + 1)
                nc.vector.tensor_tensor(mix_lo[:, p, :], B[6 + p % 2][:, 0:S], mix_hi[:, p, :].bitcast(F32),
                                        ALU.subtract).then_inc(o2_ready, 1)

            def conv(i):
                dve.wait_ge(chunk_done, 3 * t + 11 + i)
                dve.wait_ge(proj_evac, 8 * DEPTH + 10)
                nc.vector.tensor_tensor(vpad[:, 2 * i:2 * i + 2, 2:S + 2],
                                        B[i][:, :].rearrange("p (m n) -> p m n", m=2), gate_c[:, 2 * i:2 * i + 2, :],
                                        ALU.mult).then_inc(cx_evac, 1)
                dve.wait_ge(cx_evac, i + 1)
                dve.wait_ge(pads_ready, 1)
                for n in (2 * i, 2 * i + 1):
                    y = conv_y[:, n, :]
                    tap = [cp[:, CONV_W + 4 * w + n:CONV_W + 4 * w + n + 1] for w in range(3)]
                    nc.vector.tensor_scalar(y, vpad[:, n, 0:S], tap[0], None, ALU.mult).then_inc(conv_step, 1)
                    for w in (1, 2):
                        dve.wait_ge(conv_step, 4 * n + w)
                        nc.vector.scalar_tensor_tensor(y, vpad[:, n, w:w + S], tap[w], y, ALU.mult, ALU.add)\
                            .then_inc(conv_step, 1)
                    dve.wait_ge(conv_step, 4 * n + 3)
                    nc.vector.tensor_tensor(y, y, gate_b[:, n, :], ALU.mult).then_inc(conv_step, 1)

            for s in range(13):
                if 3 <= s < HEADS + 3:
                    subtract_remainder(s - 3)
                if 1 <= s <= HEADS:
                    softplus(s - 1)
                if 3 <= s < HEADS + 3:
                    mask_a(s - 3)
                if s >= 6 and s % 2 == 0:
                    heads_lo((s - 6) // 2)
                if s % 2 == 1:
                    j = 6 + s // 2
                    if j < 10:
                        dve.wait_ge(chunk_done, 3 * t + j + 1)
                        out = (gate_b if j < 8 else gate_c)[:, 2 * (j % 2):2 * (j % 2) + 2, :]
                        nc.vector.tensor_copy(out, B[j % 2][:, :].rearrange("p (m n) -> p m n", m=2))\
                            .then_inc(proj_evac, 1)
                    else:
                        conv(j - 10)
                    split(t, j + 3)
            for n in range(4):
                dve.wait_ge(conv_hi, n + 1)
                nc.vector.tensor_tensor(mix_lo[:, 4 + n, :], conv_y[:, n, :], mix_hi[:, 4 + n, :].bitcast(F32),
                                        ALU.subtract).then_inc(conv_ready, 1)
            for j in range(12, 20):
                split(t, j + 3)
            for j, banks in ((20, B[2:4]), (21, B[4:6])):
                dve.wait_ge(chunk_done, 3 * t + j + 1)
                dve.wait_ge(proj_evac, 8 * DEPTH + 18)
                for q in range(2):
                    p = 2 * (j - 20) + q
                    nc.vector.tensor_tensor(branch[:, 2 * p:2 * p + 2, :],
                                            banks[q][:, :].rearrange("p (m n) -> p m n", m=2),
                                            sig_a[:, 2 * p:2 * p + 2, :], ALU.mult).then_inc(branch_a, 1)
                split(t, j + 3)
            for j, banks in ((22, B[6:8]), (23, B[0:2])):
                dve.wait_ge(chunk_done, 3 * t + j + 1)
                for q in range(2):
                    p = 2 * (j - 22) + q
                    nc.vector.tensor_tensor(sig_b[:, 2 * p:2 * p + 2, :],
                                            banks[q][:, :].rearrange("p (m n) -> p m n", m=2),
                                            sig_b[:, 2 * p:2 * p + 2, :], ALU.mult).then_inc(branch_b, 1)
                if j == 22:
                    split(t, j + 3)
                for q in range(2):
                    p = 2 * (j - 22) + q
                    dve.wait_ge(branch_a, p + 1)
                    dve.wait_ge(branch_b, p + 1)
                    nc.vector.tensor_tensor(branch[:, 2 * p:2 * p + 2, :], branch[:, 2 * p:2 * p + 2, :],
                                            sig_b[:, 2 * p:2 * p + 2, :], ALU.add).then_inc(merged_done, 1)
                for q in range(2):
                    p = 2 * (j - 22) + q
                    dve.wait_ge(merged_done, p + 1)
                    dve.wait_ge(merged_hi, p + 1)
                    nc.vector.tensor_tensor(x_lo[:, 2 * p:2 * p + 2, :], branch[:, 2 * p:2 * p + 2, :],
                                            x_hi[:, 2 * p:2 * p + 2, :].bitcast(F32), ALU.subtract)\
                        .then_inc(merged_ready, 1)
                if j == 23:
                    split(t, j + 3)
            dve.wait_ge(mods_step, 6)
            residual_sums_of_pairs(7, 1, t, 24, rms=True)
            modulated_norm(7, 2)
            split(t, 30)
            ffn(MIX_T, MIX_CHUNKS, 3, False, final=True)
            residual_sums(8, 2, after_down(MIX_T, MIX_CHUNKS + 3 * FT - 1, 3), rms=True)

            norm_stats(8, RMS_EPS, True)
            dve.wait_ge(std_ready, 9)
            nc.vector.reciprocal(rstd[:, :], rstd[:, :]).then_inc(rstd_ready, 1)
            dve.wait_ge(rstd_ready, 9)
            for k in range(KT):
                nc.vector.scalar_tensor_tensor(state[:, k, 1, :], state[:, k, 0, :],
                                               cp[:, FINAL_G + k:FINAL_G + k + 1], rstd[:, :], ALU.mult,
                                               ALU.mult).then_inc(out_ready, 1)


def _tiles(w, kt, cols):
    k, n = w.shape
    a = w.reshape(k // (kt * P), kt, P, n // cols, cols)
    return a.transpose(0, 3, 2, 1, 4).reshape(-1, P, kt * cols)


def _ffn_chunks(w_gu, w_down):
    gate, up, down = _tiles(w_gu[:, :FF], KT, 256), _tiles(w_gu[:, FF:], KT, 256), _tiles(w_down, 2, D)
    order = [gate[0], up[0], gate[1], up[1], down[0]]
    for i in range(2, FT):
        order += [gate[i], up[i], down[i - 1]]
    return order + [down[FT - 1]]


def _columns(v):
    return np.asarray(v).reshape(-1, P).T


def _consts():
    i = np.arange(P)
    c32 = np.zeros((P, CONST_COLS), np.float32)
    c32[:, IDENT:IDENT + P] = np.eye(P)
    c32[:, ONES_D:ONES_D + P] = 1.0 / D
    c32[:, TRI:TRI + P] = i[:, None] > i[None, :]
    c32[:, ONES:ONES + P] = 1.0
    valid = i[:, None] < i[None, :]
    c32[:, MASK:MASK + P] = valid
    c32[:, MASK + P:MASK + 2 * P] = 1.0
    c32[:, MASK + 2 * P:MASK + 3 * P] = valid
    s = np.arange(S)
    angle = 2 * np.pi * ((s[:, None] * s[None, :]) % S) / S
    table = np.concatenate([np.cos(angle), np.sin(angle)], 1) / math.sqrt(S)
    c32[:, DFT_S:DFT_S + 4 * S] = table.reshape(2, P, 2 * S).transpose(1, 0, 2).reshape(P, 4 * S)
    angle = 2 * np.pi * ((i[:, None] * i[None, :]) % P) / P
    c32[:, DFT_C:DFT_C + P] = np.cos(angle) / math.sqrt(P)
    c32[:, DFT_C + P:DFT_C + 2 * P] = -np.sin(angle) / math.sqrt(P)
    c16 = np.zeros((P, CONST16_COLS), np.float32)
    for m in range(2):
        c16[:, DIST + m * S:DIST + (m + 1) * S] = np.abs(m * P + i[:, None] - s[None, :])
    for h in range(HEADS):
        c16[:, SLOPES + h * P:SLOPES + (h + 1) * P] = -(2.0 ** (-8.0 * (h + 1) / HEADS)) * np.eye(P)
    return c32, c16


def kernel(**inputs):
    import concourse.bacc as bacc
    import ml_dtypes
    from concourse.bass_utils import run_bass_kernel_spmd

    a = {k: np.asarray(v) for k, v in inputs.items()}
    chunks = []
    for l in range(DEPTH):
        w_in = _tiles(a["w_in"][l], KT, 256)
        q, k, v, u = w_in[0:2], w_in[2:4], w_in[4:6], w_in[6:8]
        chunks += [v[0], v[1], q[0], k[0], q[1], k[1], u[0], u[1]]
        chunks += list(_tiles(a["w_o"][l], KT, 256))
        chunks += _ffn_chunks(a["w_gu"][l], a["w_down"][l])
    chunks += _ffn_chunks(a["ffn1_w_gu_2"][0], a["ffn1_w_down_2"][0])
    m = _tiles(a["w_mix_in_2"][0], KT, 256)
    cb, cc, cx, q, k, v, ga, gb = m[0:2], m[2:4], m[4:6], m[6:8], m[8:10], m[10:12], m[12:16], m[16:20]
    chunks += [v[0], v[1], q[0], k[0], q[1], k[1], *cb, *cc, *cx, *ga, *gb]
    chunks += list(_tiles(a["w_conv_out_2"][0], 4, 512)) + list(_tiles(a["w_attn_out_2"][0], 4, 512))
    chunks += list(_tiles(a["w_out_2"][0], KT, 256))
    chunks += _ffn_chunks(a["ffn2_w_gu_2"][0], a["ffn2_w_down_2"][0])
    stream = np.stack(chunks)
    assert stream.shape == (N_CHUNKS, P, CH)

    layer_params = np.zeros((DEPTH, P, LAYER_COLS), np.float32)
    for l in range(DEPTH):
        lam_init = 0.8 - 0.6 * math.exp(-0.3 * l)
        rows = a["lam_params"][l]
        for at, v in ((LN1_G, a["ln1_g"][l]), (LN1_B, a["ln1_b"][l]), (LN2_G, a["ln2_g"][l]),
                      (LN2_B, a["ln2_b"][l]), (B_F, a["b_f"][l])):
            layer_params[l, :, at:at + v.size // P] = _columns(v)
        layer_params[l, :, SUBLN] = np.concatenate([a["subln_g"][l]] * 2)
        layer_params[l, :, ONE_MINUS_LI] = 1.0 - lam_init
        layer_params[l, :, LAM_INIT] = lam_init
        layer_params[l, :, LAM_ROWS:] = np.concatenate([rows[0], rows[2], rows[1], rows[3]])[None, :]
    common = np.concatenate([_columns(a[n]) for n in (
        "ln_in_g", "ln_in_b", "c_2", "b_ada_2", "norm1_g_2", "norm2_g_2", "norm3_g_2", "b_merge_2", "conv_w_2",
        "final_g_2")], 1)
    assert common.shape == (P, COMMON_COLS)
    consts32, consts16 = _consts()
    arrays = {
        "xT": a["x"][0].T,
        "stream": stream,
        "ada": a["w_ada_2"][0].reshape(KT, P, ADA_TILES, ADA_COLS).transpose(2, 1, 0, 3),
        "w_f": a["w_f"],
        "layer_params": layer_params,
        "common_params": common,
        "consts32": consts32,
        "consts16": consts16.astype(ml_dtypes.bfloat16),
    }
    arrays = {k: np.ascontiguousarray(v) for k, v in arrays.items()}
    nc = bacc.Bacc("TRN2", target_bir_lowering=False, num_devices=1)
    ins = [nc.dram_tensor(k, v.shape, mybir.dt.from_np(v.dtype), kind="ExternalInput").ap() for k, v in arrays.items()]
    outT = nc.dram_tensor("outT", (D, S), F32, kind="ExternalOutput").ap()
    fused_blocks(nc, *ins, outT)
    r = run_bass_kernel_spmd(nc, [arrays], core_ids=[0])
    return np.ascontiguousarray(r.results[0]["outT"].T)[None]
```
